# Optimizing a Trainium2 kernel written in Bass

```python
import jax, jax.numpy as jnp
from jax import lax
import numpy as np

D_MODEL = 1024
BATCH = 1
SEQ = 512
DEPTH = 2

CHUNK = 64
N_A_LAYERS = max(1, DEPTH // 2)
N_B_LAYERS = DEPTH - N_A_LAYERS
CONV_WIDTH = 3
N_HEADS = 16
HEAD_DIM = D_MODEL // N_HEADS
Q_BLOCK = 128
PEER_HEADS = 8
PEER_N_KEYS = 128
PEER_N_EXPERTS = PEER_N_KEYS ** 2
PEER_D_KEY = 256
PEER_HALF = PEER_D_KEY // 2
PEER_TOPK = 16
PEER_TOKEN_BLOCK = 128
RMS_EPS = 1e-6

kernel_name = "yoco_shortconv_fox_peer_adaln"

def rmsnorm(x, gain):
    xf = x.astype(jnp.float32)
    y = xf * lax.rsqrt(jnp.mean(xf * xf, axis=-1, keepdims=True) + RMS_EPS)
    return (y * gain.astype(jnp.float32)).astype(x.dtype)

def ada_params(c, w, b, n):
    m = jax.nn.silu(c) @ w + b
    return [t[:, None, :] for t in jnp.split(m, n, axis=-1)]

def modulate(h, shift, scale):
    return h * (1 + scale) + shift

def short_conv_mixer(h, w_in, conv_w, w_out):
    b_gate, c_gate, u = jnp.split(h @ w_in, 3, axis=-1)
    z = lax.conv_general_dilated(
        c_gate * u, conv_w[:, None, :], window_strides=(1,),
        padding=[(CONV_WIDTH - 1, 0)], dimension_numbers=('NWC', 'WIO', 'NWC'),
        feature_group_count=D_MODEL)
    return (b_gate * z) @ w_out

def shared_kv(x, c, gain, ada_w, ada_b, w_kvf, f_bias):
    shift, scale = ada_params(c, ada_w, ada_b, 2)
    h = modulate(rmsnorm(x, gain), shift, scale)
    b_, s_ = x.shape[:2]
    k, v, f_logit = jnp.split(h @ w_kvf, [D_MODEL, 2 * D_MODEL], axis=-1)
    k = k.reshape(b_, s_, N_HEADS, HEAD_DIM).transpose(0, 2, 1, 3)
    v = v.reshape(b_, s_, N_HEADS, HEAD_DIM).transpose(0, 2, 1, 3)
    log_f = jax.nn.log_sigmoid((f_logit + f_bias).astype(jnp.float32))
    cum_f = lax.cumsum(log_f, axis=1).transpose(0, 2, 1)
    return k, v, cum_f

def forgetting_attention(h, w_q, w_o, k, v, cum_f):
    b_, s_ = h.shape[:2]
    q = (h @ w_q).reshape(b_, s_, N_HEADS, HEAD_DIM).transpose(0, 2, 1, 3)
    scale = HEAD_DIM ** -0.5
    outs = []
    for qs in range(0, s_, Q_BLOCK):
        ke = qs + Q_BLOCK
        logits = jnp.einsum('bhqd,bhkd->bhqk', q[:, :, qs:ke], k[:, :, :ke]).astype(jnp.float32) * scale
        logits = logits + cum_f[:, :, qs:ke, None] - cum_f[:, :, None, :ke]
        q_pos = qs + jnp.arange(Q_BLOCK)
        k_pos = jnp.arange(ke)
        logits = jnp.where(k_pos[None, :] <= q_pos[:, None], logits, -jnp.inf)
        p = jax.nn.softmax(logits, axis=-1).astype(v.dtype)
        outs.append(jnp.einsum('bhqk,bhkd->bhqd', p, v[:, :, :ke]))
    o = jnp.concatenate(outs, axis=2).transpose(0, 2, 1, 3).reshape(b_, s_, D_MODEL)
    return o @ w_o

def peer(h, w_q, sub_keys, u, v):
    b_, s_, d = h.shape
    t = b_ * s_
    ht = h.reshape(t, d)
    q = (ht @ w_q).reshape(t, PEER_HEADS, 2, PEER_HALF)
    sub_scores = jnp.einsum('thpd,hpkd->thpk', q, sub_keys).astype(jnp.float32)
    s_top, i_top = lax.top_k(sub_scores, PEER_TOPK)
    cand_s = (s_top[:, :, 0, :, None] + s_top[:, :, 1, None, :]).reshape(t, PEER_HEADS, PEER_TOPK * PEER_TOPK)
    cand_i = (i_top[:, :, 0, :, None] * PEER_N_KEYS + i_top[:, :, 1, None, :]).reshape(t, PEER_HEADS, PEER_TOPK * PEER_TOPK)
    best_s, best_pos = lax.top_k(cand_s, PEER_TOPK)
    expert_idx = jnp.take_along_axis(cand_i, best_pos, axis=-1)
    gates = jax.nn.softmax(best_s, axis=-1).astype(h.dtype)
    n_blk = t // PEER_TOKEN_BLOCK
    n_sel = PEER_HEADS * PEER_TOPK

    def block(args):
        xb, ib, gb = args
        ub = jnp.take(u, ib, axis=0)
        vb = jnp.take(v, ib, axis=0)
        act = jax.nn.gelu(jnp.einsum('td,ted->te', xb, ub))
        return jnp.einsum('te,ted->td', gb * act, vb)

    out = lax.map(block, (ht.reshape(n_blk, PEER_TOKEN_BLOCK, d),
                          expert_idx.reshape(n_blk, PEER_TOKEN_BLOCK, n_sel),
                          gates.reshape(n_blk, PEER_TOKEN_BLOCK, n_sel)))
    return out.reshape(b_, s_, d)

def setup_inputs(seed: int = 0) -> dict:
    key = jax.random.key(seed)
    ks = jax.random.split(key, 23)
    d = D_MODEL
    nrm = jax.random.normal
    inv = d ** -0.5
    return {
        "x": nrm(ks[0], (BATCH, SEQ, d), jnp.float32),
        "c": nrm(ks[1], (BATCH, d), jnp.float32),
        "mix_norm": 1.0 + 0.05 * nrm(ks[2], (DEPTH, d), jnp.float32),
        "mix_ada_w": 0.2 * inv * nrm(ks[3], (DEPTH, d, 3 * d), jnp.float32),
        "mix_ada_b": 0.02 * nrm(ks[4], (DEPTH, 3 * d), jnp.float32),
        "ffn_norm": 1.0 + 0.05 * nrm(ks[5], (DEPTH, d), jnp.float32),
        "ffn_ada_w": 0.2 * inv * nrm(ks[6], (DEPTH, d, 3 * d), jnp.float32),
        "ffn_ada_b": 0.02 * nrm(ks[7], (DEPTH, 3 * d), jnp.float32),
        "a_w_in": inv * nrm(ks[8], (N_A_LAYERS, d, 3 * d), jnp.float32),
        "a_conv": (CONV_WIDTH ** -0.5) * nrm(ks[9], (N_A_LAYERS, CONV_WIDTH, d), jnp.float32),
        "a_w_out": inv * nrm(ks[10], (N_A_LAYERS, d, d), jnp.float32),
        "kv_norm": 1.0 + 0.05 * nrm(ks[11], (d,), jnp.float32),
        "kv_ada_w": 0.2 * inv * nrm(ks[12], (d, 2 * d), jnp.float32),
        "kv_ada_b": 0.02 * nrm(ks[13], (2 * d,), jnp.float32),
        "kv_w": inv * nrm(ks[14], (d, 2 * d + N_HEADS), jnp.float32),
        "f_bias": jax.random.uniform(ks[15], (N_HEADS,), jnp.float32, 2.0, 7.0),
        "b_w_q": inv * nrm(ks[16], (N_B_LAYERS, d, d), jnp.float32),
        "b_w_o": inv * nrm(ks[17], (N_B_LAYERS, d, d), jnp.float32),
        "peer_w_q": inv * nrm(ks[18], (DEPTH, d, PEER_HEADS * PEER_D_KEY), jnp.float32),
        "peer_sub_keys": (PEER_HALF ** -0.5) * nrm(ks[19], (DEPTH, PEER_HEADS, 2, PEER_N_KEYS, PEER_HALF), jnp.float32),
        "peer_u": inv * nrm(ks[20], (DEPTH, PEER_N_EXPERTS, d), jnp.float32),
        "peer_v": (PEER_HEADS ** -0.5) * nrm(ks[21], (DEPTH, PEER_N_EXPERTS, d), jnp.float32),
        "final_norm": 1.0 + 0.05 * nrm(ks[22], (d,), jnp.float32),
    }

def reference(x, c, mix_norm, mix_ada_w, mix_ada_b, ffn_norm, ffn_ada_w, ffn_ada_b,
              a_w_in, a_conv, a_w_out, kv_norm, kv_ada_w, kv_ada_b, kv_w, f_bias,
              b_w_q, b_w_o, peer_w_q, peer_sub_keys, peer_u, peer_v, final_norm):
    kv = None
    for layer in range(DEPTH):
        shift, scale, gate = ada_params(c, mix_ada_w[layer], mix_ada_b[layer], 3)
        h = modulate(rmsnorm(x, mix_norm[layer]), shift, scale)
        if layer < N_A_LAYERS:
            y = short_conv_mixer(h, a_w_in[layer], a_conv[layer], a_w_out[layer])
        else:
            j = layer - N_A_LAYERS
            y = forgetting_attention(h, b_w_q[j], b_w_o[j], kv[0], kv[1], kv[2])
        x = x + (1 + gate) * y
        shift, scale, gate = ada_params(c, ffn_ada_w[layer], ffn_ada_b[layer], 3)
        h = modulate(rmsnorm(x, ffn_norm[layer]), shift, scale)
        x = x + (1 + gate) * peer(h, peer_w_q[layer], peer_sub_keys[layer], peer_u[layer], peer_v[layer])
        if layer == N_A_LAYERS - 1:
            kv = shared_kv(x, c, kv_norm, kv_ada_w, kv_ada_b, kv_w, f_bias)
    return rmsnorm(x, final_norm)


_drawn_inputs = setup_inputs


def setup_inputs(seed=0):
    import zlib

    import numpy as np

    out = dict(_drawn_inputs(seed))
    spreads = {}
    factors = {'kv_norm': 3.706, 'kv_ada_b': 2.776}
    for name, (base, spread) in spreads.items():
        noise = np.random.default_rng([zlib.crc32(name.encode()), seed]).standard_normal(out[name].shape)
        drawn = base * np.exp(spread * noise) if base else spread * noise
        out[name] = __import__('jax').numpy.asarray(drawn.astype(out[name].dtype))
    for name, factor in factors.items():
        out[name] = (out[name] * factor).astype(out[name].dtype)
    return out
```

```python
from contextlib import ExitStack

import concourse.bass as bass
from concourse import mybir

ALU = mybir.AluOpType
ACT = mybir.ActivationFunctionType
F32 = mybir.dt.float32
U32 = mybir.dt.uint32
AX_X = mybir.AxisListType.X

P = 128
D = 1024
S = 512
NT = S // P
KB = D // P
HEADS = 16
HD = D // HEADS
PH = 8
NK = 128
DK = 128
TOPK = 16
LISTS = 2 * PH
SLOTS = PH * TOPK
CW = 256
EPS = 1e-6
LOWEST = -3.0e38
FR = 112

N_ADA = (6 * D // CW, 8 * D // CW)
N_IN = 3 * D // CW
N_SQ = D // CW
N_PQ = 2 * D // CW
N_KQ = 2 * D // CW
C_ADA0 = 0
C_IN = C_ADA0 + N_ADA[0]
C_OUT = C_IN + N_IN
C_PQ0 = C_OUT + N_SQ
C_ADA1 = C_PQ0 + N_PQ
C_V = C_ADA1 + N_ADA[1]
C_KQ = C_V + N_SQ
C_WO = C_KQ + N_KQ
C_PQ1 = C_WO + N_SQ
N_CHUNKS = C_PQ1 + N_PQ

SHIFT, SCALE, GATE, KV_SHIFT, KV_SCALE, F_SHIFT, F_SCALE, F_GATE1, F_GATE0 = range(9)
F_GATE = (F_GATE0, F_GATE1)

K_ID, K_MASK, K_IOTA, K_SEL, K_ONE = 0, 128, 256, 272, 288
K_COLS = 289

HALF = 4
STEPS = SLOTS // HALF


class Ticks:

    def __init__(self, eng, sem):
        self.eng, self.sem, self.n, self.turn, self.per, self.start = eng, sem, 0, None, 0, 0

    def __call__(self, ins):
        ins.then_inc(self.sem, 1)
        self.n += 1

    def sync(self, back=0):
        n = self.n - back
        self.eng.wait_ge(self.sem, n if self.turn is None else self.turn * self.per + n)

    def enter(self, turn, per):
        self.turn, self.per, self.start = turn, per, self.n

    def leave(self, times):
        assert self.n - self.start == self.per, (self.n - self.start, self.per)
        self.n = self.start + self.per * times
        self.turn = None


def peeled(eng, times, body):
    body(0, True)
    if times > 1:
        with eng.Fori(1, times) as i:
            body(i, False)


def bass_trunk(nc, x, cT, consts, conv, f_w, f_bias, bias_rows, gains, keys, wstream, tables, out):
    with ExitStack() as ctx:
        def sb(name, shape, dt=F32):
            return ctx.enter_context(nc.sbuf_tensor(name, shape, dt))

        def sem(name):
            return ctx.enter_context(nc.semaphore(name))

        xs = sb("xs", [P, NT, D])
        hs = sb("hs", [P, NT, D])
        hT = sb("hT", [P, KB, S])
        rows = sb("rows", [P, 9, D])
        ring = sb("ring", [P, 16, D])
        wring = sb("wring", [P, 2, KB, CW])
        sc = sb("sc", [P, NT, LISTS, NK])
        kc = sb("kc", [P, K_COLS])
        cs = sb("cs", [P, 3, KB])
        sB = sb("sB", [P, KB, P])
        convs = sb("convs", [P, KB, 3])
        taps = sb("taps", [P, 2, 3])
        stat = sb("stat", [P, 2, NT])
        fb = sb("fb", [FR, 1])
        fw = sb("fw", [P, KB, FR])
        idx = sb("idx", [P, 2, SLOTS], U32)
        gates = sb("gates", [P, 2, SLOTS])
        gsum = sb("gsum", [P, 2, PH])
        idx_u = sb("idx_u", [P, 2, HALF], U32)
        idx_v = sb("idx_v", [P, 2, HALF], U32)
        dots = sb("dots", [P, 2, HALF])
        acts = sb("acts", [P, 2, HALF])
        coef = sb("coef", [P, 2, HALF])
        amax = sb("amax", [P, 2, NT])
        asum = sb("asum", [P, 2, NT])
        ainv = sb("ainv", [P, 2, NT])
        psum = ctx.enter_context(nc.psum_tensor("psum", [P, 8, 512], F32))
        ps = [psum[:, b, :] for b in range(8)]
        acc = psum[:, 6:8, :].rearrange("p a b -> p (a b)")

        ident = kc[:, K_ID:K_ID + P]
        mask = kc[:, K_MASK:K_MASK + P]
        iota = kc[:, K_IOTA:K_IOTA + TOPK]
        one = kc[:, K_ONE:K_ONE + 1]

        brow = ring[:, 0:8, :]
        gain = ring[:, 8:11, :]
        keyT = ring[:, 14:16, :].rearrange("p a b -> p (a b)")
        c_s = ring[:, 10, :].rearrange("p (j t) -> p j t", j=2)
        cu = ring[:, 11:13, :].rearrange("p a b -> p (a b)")[:, 0:2 * (S + 2)].rearrange("p (j t) -> p j t", j=2)
        z_s = ring[:, 13, :].rearrange("p (j t) -> p j t", j=2)
        y_s = ring[:, 12:14, :].rearrange("p s (t n) -> p s t n", t=NT)
        qs = ring[:, 1, :].rearrange("p (j t) -> p j t", j=2)
        gT = hs[:].rearrange("p t n -> p (t n)").rearrange("p (k t) -> p k t", k=KB)
        hqT = ring[:, 0:4, :].rearrange("p a b -> p (a b)").rearrange("p (k t) -> p k t", k=KB)
        vs = ring[:, 4:8, :]
        kqs = ring[:, 11:13, :].rearrange("p a (b t) -> p a b t", b=2)

        scf = sc[:].rearrange("p a b c -> p (a b c)")
        cum = scf[0:FR, 0:512]
        aux_r = scf[0:FR, 512:1024]
        aux_b = scf[0:FR, 1024:1536]
        aux_l = scf[0:FR, 1536:2048]
        T_OFF = [0, 128, 384, 768]
        prob = scf[:, 2560:5120].rearrange("p (a b) -> p a b", a=2)
        probT = scf[:, 5120:6400]

        hf = hT[:].rearrange("p a b -> p (a b)")
        cand = hf[:, 0:1024].rearrange("p (h a b) -> p h a b", h=4, a=TOPK)
        candf = hf[:, 0:1024].rearrange("p (h c) -> p h c", h=4)
        eq = hf[:, 1024:2048]
        stage = hf[:, 1024:1536].rearrange("p (l k) -> p l k", l=4)
        tv = hf[:, 2048:2304].rearrange("p (l k) -> p l k", l=LISTS)
        tif = hf[:, 2304:2560].rearrange("p (l k) -> p l k", l=LISTS)
        tv4 = hf[:, 2560:2624].rearrange("p (l k) -> p l k", l=4)
        ti4 = hf[:, 2624:2688].rearrange("p (l k) -> p l k", l=4).bitcast(U32)
        bv4 = hf[:, 2688:2752].rearrange("p (l k) -> p l k", l=4)
        bp4 = hf[:, 2752:2816].bitcast(U32)
        ra4 = hf[:, 2816:2880].bitcast(U32)
        rb4 = hf[:, 2880:2944].bitcast(U32)
        e1 = hf[:, 2944:3008]
        e2 = hf[:, 3008:3072]
        bs = hf[:, 3072:3200].rearrange("p (h k) -> p h k", h=PH)
        bd = hf[:, 3200:3328].rearrange("p (h k) -> p h k", h=PH)

        names = ("x c const conv fw fb bias0 gain0 keys0 bias1 gain1 keys1 gainf").split()
        ld = {n: sem("ld_" + n) for n in names}
        w_got = [sem(f"w_got{s}") for s in range(2)]
        w_used = [sem(f"w_used{s}") for s in range(2)]
        dv, av = sem("dv"), sem("av")
        silu_e, silu_b = sem("silu_e"), sem("silu_b")
        ada_out = [sem(f"ada_out{i}") for i in range(2)]
        rows_ok = [sem(f"rows_ok{i}") for i in range(2)]
        x_mix = [sem(f"x_mix{i}") for i in range(2)]
        x_ffn = [sem(f"x_ffn{i}") for i in range(2)]
        NORMS = ["mix0", "ffn0", "kv", "mix1", "ffn1", "fin"]
        n_sq = {n: sem(f"sumsq_{n}") for n in NORMS}
        n_ms = {n: sem(f"meansq_{n}") for n in NORMS}
        n_rt = {n: sem(f"root_{n}") for n in NORMS}
        n_h = {n: sem(f"h_{n}") for n in NORMS}
        n_tr = {n: sem(f"tr_{n}") for n in NORMS + ["att"]}
        n_hT = {n: sem(f"hT_{n}") for n in NORMS + ["att"]}
        c_out, cu_ok, g_ok = sem("c_out"), sem("cu_ok"), sem("g_ok")
        y_in = [sem(f"y_in{i}") for i in range(2)]
        q_out = [sem(f"q_out{i}") for i in range(2)]
        s_done = [sem(f"s_done{i}") for i in range(2)]
        s_out = [sem(f"s_out{i}") for i in range(2)]
        f_done, f_z, f_l = sem("f_done"), sem("f_z"), sem("f_l")
        v_out = sem("v_out")
        k_out = sem("k_out")
        aux_ok, a_s, a_max, a_exp = sem("aux_ok"), sem("a_s"), sem("a_max"), sem("a_exp")
        a_tr, a_trc, a_pv, a_o = sem("a_tr"), sem("a_trc"), sem("a_pv"), sem("a_o")
        r_d, r_e, r_ok = sem("r_d"), sem("r_e"), sem("r_ok")
        u_got = [sem(f"u_got{n}") for n in range(2)]
        v_got = [sem(f"v_got{n}") for n in range(2)]
        u_used = [sem(f"u_used{n}") for n in range(2)]
        v_used = [sem(f"v_used{n}") for n in range(2)]
        ix_u, ix_v = sem("ix_u"), sem("ix_v")
        act_ok = [sem(f"act_ok{n}") for n in range(2)]
        y_ok, stored, cu_0 = sem("y_ok"), sem("stored"), sem("cu_0")

        block = ctx.enter_context(nc.Block())

        def w_ready(eng, n, i=0):
            eng.wait_ge(w_got[n % 2], 16 * (n // 2 + 1) + 16 * i)

        def w_done(eng, n, i=0):
            eng.wait_ge(w_used[n % 2], n // 2 + 1 + i)

        @block.sync
        def _(sp):
            def chunks(i, first):
                for s in range(2):
                    if not first:
                        sp.wait_ge(w_used[s], i)
                    sp.dma_start(wring[:, s].rearrange("p k n -> p (k n)"),
                                 wstream[2 * i + s]).then_inc(w_got[s], 16)
            peeled(sp, N_CHUNKS // 2, chunks)
            sp.wait_ge(y_ok, NT)
            sp.dma_start(out.rearrange("(t p) d -> p t d", p=P), xs[:]).then_inc(stored, 16)
            sp.wait_ge(stored, 16)

        @block.tensor
        def _(pe):
            def ada(which, c0, n):
                def body(i, first):
                    for s in range(2):
                        w_ready(pe, c0 + s, i)
                        if not first:
                            pe.wait_ge(ada_out[which], 2 * i - 1 + s)
                        for k in range(KB):
                            mm = pe.matmul(ps[s][:, 0:CW], sB[:, k, :], wring[:, s, k, :],
                                           start=(k == 0), stop=(k == KB - 1))
                        mm.then_inc(w_used[s], 1)
                peeled(pe, n // 2, body)

            def transposes(name, src, ready):
                for t in range(NT):
                    ready(t)
                    for half in range(2):
                        b = 4 + 2 * (t % 2) + half
                        if t >= 2:
                            pe.wait_ge(n_hT[name], 2 * (t - 2) + half + 1)
                        for j in range(4):
                            k = 4 * half + j
                            mm = pe.transpose(ps[b][:, j * P:(j + 1) * P], src[:, t, k * P:(k + 1) * P], ident)
                        mm.then_inc(n_tr[name], 1)

            def norm_T(name):
                transposes(name, hs, lambda t: pe.wait_ge(n_h[name], t + 1))

            def in_proj():
                pe.wait_ge(n_hT["mix0"], 2 * NT)
                pe.wait_ge(ada_out[0], N_ADA[0])

                def body(i, first):
                    for jp in range(2):
                        for third in range(3):
                            n = C_IN + 3 * jp + third
                            w_ready(pe, n, 3 * i)
                            if not (first and jp == 0):
                                s_free = (c_out, cu_ok, g_ok)[third]
                                pe.wait_ge(s_free, 4 * i + 2 * jp)
                            for jj in range(2):
                                for k in range(KB):
                                    mm = pe.matmul(ps[2 * third + jj], wring[:, n % 2, k, jj * P:(jj + 1) * P],
                                                   hT[:, k, :], start=(k == 0), stop=(k == KB - 1))
                            mm.then_inc(w_used[n % 2], 1)
                peeled(pe, 2, body)

            def project(src, c0, free):
                def body(i, first):
                    for s in range(2):
                        w_ready(pe, c0 + s, i)
                        for t in range(NT):
                            if not first:
                                pe.wait_ge(free, 4 * (2 * i + s - 2) + t + 1)
                            for k in range(KB):
                                mm = pe.matmul(ps[4 * s + t][:, 0:CW], src[:, k, t * P:(t + 1) * P],
                                               wring[:, s, k, :], start=(k == 0), stop=(k == KB - 1))
                        mm.then_inc(w_used[s], 1)
                peeled(pe, N_SQ // 2, body)

            def peer_scores(L, c0):
                name = f"ffn{L}"
                pe.wait_ge(n_hT[name], 2 * NT)
                pe.wait_ge(ld[f"keys{L}"], 16)

                def body(i, first):
                    for s in range(2):
                        w_ready(pe, c0 + s, i)
                        n2 = 2 * s
                        for b in range(2):
                            if not (first and s == 0):
                                pe.wait_ge(q_out[L], 4 * i + n2 - 1 + b)
                            for k in range(KB):
                                mm = pe.matmul(ps[b], wring[:, s, k, b * P:(b + 1) * P], hT[:, k, :],
                                               start=(k == 0), stop=(k == KB - 1))
                        mm.then_inc(w_used[s], 1)
                        for b in range(2):
                            pe.wait_ge(q_out[L], 4 * i + n2 + b + 1)
                            if not (first and s == 0):
                                pe.wait_ge(s_out[L], 4 * i + n2 - 1 + b)
                            for t in range(NT):
                                mm = pe.matmul(ps[2 + b][:, t * P:(t + 1) * P], qs[:, b, t * P:(t + 1) * P],
                                               keyT[:, bass.ds((4 * i + n2 + b) * NK, NK)], start=True, stop=True)
                            mm.then_inc(s_done[L], 1)
                peeled(pe, N_PQ // 2, body)

            def forget():
                pe.wait_ge(n_hT["kv"], 2 * NT)
                pe.wait_ge(ld["fw"], 16)
                pe.wait_ge(ada_out[1], N_ADA[1])
                for k in range(KB):
                    mm = pe.matmul(ps[0][0:FR, :], fw[:, k, :], hT[:, k, :], start=(k == 0), stop=(k == KB - 1))
                mm.then_inc(f_done, 1)

            def attention():
                pe.wait_ge(n_hT["mix1"], 2 * NT)
                pe.wait_ge(v_out, 4 * N_SQ)

                def kq(i, s, first):
                    w_ready(pe, C_KQ + s, i)
                    if not (first and s == 0):
                        pe.wait_ge(a_o, 4 * i + 2 * s - 1)
                    for k in range(KB):
                        pe.matmul(ps[0], wring[:, s, k, 0:P], hT[:, k, :], start=(k == 0), stop=(k == KB - 1))
                    if not (first and s == 0):
                        pe.wait_ge(a_o, 4 * i + 2 * s)
                    for k in range(KB):
                        mm = pe.matmul(ps[1], wring[:, s, k, P:2 * P], hqT[:, k, :],
                                       start=(k == 0), stop=(k == KB - 1))
                    mm.then_inc(w_used[s], 1)

                def scores(i, h, first):
                    s, hh = h // 2, h % 2
                    pb = 64 * hh
                    if hh == 0:
                        pe.wait_ge(k_out, 4 * i + 2 * s + 2)
                    pe.wait_ge(aux_ok, 4 * i + h + 1)
                    for t in range(NT):
                        if not (first and h == 0):
                            pe.wait_ge(a_exp, 4 * (4 * i + h - 1) + t + 1)
                        ke = (t + 1) * P
                        pe.matmul(ps[2 + t][:, 0:ke], kqs[pb:pb + 64, s, 1, t * P:ke], kqs[pb:pb + 64, s, 0, 0:ke],
                                  start=True, stop=False)
                        pe.matmul(ps[2 + t][:, 0:ke], aux_l[pb:pb + 48, t * P:ke], aux_r[pb:pb + 48, 0:ke],
                                  start=False, stop=True).then_inc(a_s, 1)

                def values(i, h, first):
                    n = 4 * i + h
                    for t in range(NT):
                        pe.wait_ge(a_exp, 4 * n + t + 1)
                        if not (first and h == 0 and t < 2):
                            pe.wait_ge(a_trc, 4 * n + t - 1)
                        for kb in range(t + 1):
                            mm = pe.transpose(ps[6 + t % 2][:, kb * P:(kb + 1) * P],
                                              prob[:, h % 2, T_OFF[t] + kb * P:T_OFF[t] + (kb + 1) * P], ident)
                        mm.then_inc(a_tr, 1)
                    if not (first and h < 2):
                        pe.wait_ge(a_o, n - 1)
                    for t in range(NT):
                        pe.wait_ge(a_trc, 4 * n + t + 1)
                        for kb in range(t + 1):
                            mm = pe.matmul(ps[h % 2][:, t * HD:(t + 1) * HD],
                                           probT[:, T_OFF[t] + kb * P:T_OFF[t] + (kb + 1) * P],
                                           vs[:, kb, bass.ds(n * HD, HD)], start=(kb == 0), stop=(kb == t))
                    mm.then_inc(a_pv, 1)

                def body(i, first):
                    for h in range(4):
                        if h % 2 == 0:
                            if not (first and h == 0):
                                values(i, h - 1, first) if h else values(i - 1, 3, False)
                            kq(i, h // 2, first)
                            scores(i, h, first)
                        else:
                            scores(i, h, first)
                            values(i, h - 1, first)
                peeled(pe, HEADS // 4, body)
                values(HEADS // 4 - 1, 3, False)

            pe.wait_ge(silu_b, 1)
            ada(0, C_ADA0, N_ADA[0])
            pe.wait_ge(ld["const"], 16)
            norm_T("mix0")
            in_proj()
            pe.wait_ge(g_ok, KB)
            project(gT, C_OUT, y_in[0])
            pe.wait_ge(y_in[0], 4 * N_SQ)
            norm_T("ffn0")
            peer_scores(0, C_PQ0)
            pe.wait_ge(s_out[0], LISTS)
            ada(1, C_ADA1, N_ADA[1])
            norm_T("kv")
            forget()
            pe.wait_ge(f_z, 1)
            project(hT, C_V, v_out)
            norm_T("mix1")
            attention()
            pe.wait_ge(a_o, HEADS)
            transposes("att", hs, lambda t: None)
            pe.wait_ge(n_hT["att"], 2 * NT)
            project(hT, C_WO, y_in[1])
            pe.wait_ge(y_in[1], 4 * N_SQ)
            norm_T("ffn1")
            peer_scores(1, C_PQ1)

        @block.scalar
        def _(act):
            def load(dst, src, name):
                act.dma_start(dst, src).then_inc(ld[name], 16)

            me = Ticks(act, av)

            flat_rows = rows[:].rearrange("p r n -> p (r n)")

            def ada_pair(which, c0, row0, i):
                for s in range(2):
                    w_done(act, c0 + s, i)
                    act.activation(flat_rows[:, bass.ds(row0 * D + (2 * i + s) * CW, CW)], ps[s][:, 0:CW],
                                   ACT.Copy).then_inc(ada_out[which], 1)

            def ada0(c0, n, row0):
                with act.Fori(0, n // 2) as i:
                    ada_pair(0, c0, row0, i)

            def copies(name, dst):
                for t in range(NT):
                    for half in range(2):
                        b = 4 + 2 * (t % 2) + half
                        act.wait_ge(n_tr[name], 2 * t + half + 1)
                        act.activation(dst[:, 4 * half:4 * half + 4, t * P:(t + 1) * P],
                                       ps[b].rearrange("p (j t) -> p j t", j=4), ACT.Copy).then_inc(n_hT[name], 1)

            def norm(name, dst, x_sem, x_count):
                act.wait_ge(x_sem, x_count)
                for t in range(NT):
                    act.activation(hs[:, t, :], xs[:, t, :], ACT.Square,
                                   accum_out=stat[:, 0, t:t + 1]).then_inc(n_sq[name], 1)
                act.wait_ge(n_ms[name], 1)
                act.activation(stat[:, 1, :], stat[:, 0, :], ACT.Sqrt).then_inc(n_rt[name], 1)
                if dst is not None:
                    copies(name, dst)

            def in_proj():
                def body(i, first):
                    for jp in range(2):
                        n = C_IN + 3 * jp
                        w_done(act, n, 3 * i)
                        if not (first and jp == 0):
                            act.wait_ge(cu_ok, 4 * i + 2 * jp)
                        for jj in range(2):
                            act.activation(c_s[:, jj, :], ps[jj], ACT.Copy).then_inc(c_out, 1)
                peeled(act, 2, body)

            def peer_scores(L, c0):
                def body(i, first):
                    for s in range(2):
                        w_done(act, c0 + s, i)
                        for b in range(2):
                            if not (first and s == 0):
                                act.wait_ge(s_done[L], 4 * i + 2 * s - 1 + b)
                            act.activation(qs[:, b, :], ps[b], ACT.Copy).then_inc(q_out[L], 1)
                        for b in range(2):
                            act.wait_ge(s_done[L], 4 * i + 2 * s + b + 1)
                            act.activation(sc[:, :, 4 * i + 2 * s + b, :], ps[2 + b].rearrange("p (t k) -> p t k", t=NT),
                                           ACT.Copy).then_inc(s_out[L], 1)
                peeled(act, N_PQ // 2, body)

            def soft(T):
                act.wait_ge(r_d, T + 1)
                act.activation(bd, bd, ACT.Exp).then_inc(r_e, 1)

            def gelus(T, with_ada=False):
                def half(n, f):
                    act.wait_ge(u_used[n], HALF * (f + 1))
                    act.activation(acts[:, n, :], dots[:, n, :], ACT.Gelu_apprx_tanh).then_inc(act_ok[n], 1)
                with act.Fori(0, STEPS // 2) as i:
                    half(0, i + T * (STEPS // 2))
                    half(1, i + T * (STEPS // 2))
                    if with_ada:
                        ada_pair(1, C_ADA1, SHIFT, i)

            def forget():
                act.wait_ge(f_z, 1)
                me(act.activation(aux_r, cum, ACT.Abs))
                me.sync()
                me(act.activation(aux_b, aux_r, ACT.Exp, scale=-1.0))
                me.sync()
                act.activation(aux_r, aux_b, ACT.Ln, bias=one[0:FR, :]).then_inc(f_l, 1)

            def project_v():
                def body(i, first):
                    for s in range(2):
                        w_done(act, C_V + s, i)
                        for t in range(NT):
                            act.activation(vs[:, t, bass.ds((2 * i + s) * CW, CW)], ps[4 * s + t][:, 0:CW],
                                           ACT.Copy).then_inc(v_out, 1)
                peeled(act, N_SQ // 2, body)

            def attention():
                def kq(i, s, first):
                    w_done(act, C_KQ + s, i)
                    if not first:
                        act.wait_ge(a_s, 16 * i + 8 * s - 8)
                    act.activation(kqs[:, s, 0, :], ps[0], ACT.Copy).then_inc(k_out, 1)
                    act.activation(kqs[:, s, 1, :], ps[1], ACT.Copy, scale=HD ** -0.5).then_inc(k_out, 1)

                def exps(i, h, first):
                    n = 4 * i + h
                    if not (first and h < 2):
                        act.wait_ge(a_tr, 4 * (n - 1))
                    for t in range(NT):
                        ke = (t + 1) * P
                        act.wait_ge(a_max, 4 * n + t + 1)
                        act.activation(prob[:, h % 2, T_OFF[t]:T_OFF[t] + ke], ps[2 + t][:, 0:ke], ACT.Exp,
                                       bias=amax[:, h % 2, t:t + 1],
                                       accum_out=asum[:, h % 2, t:t + 1]).then_inc(a_exp, 1)

                def probs_T(i, h, first):
                    n = 4 * i + h
                    if not (first and h == 0):
                        act.wait_ge(a_pv, n)
                    for t in range(NT):
                        ke = (t + 1) * P
                        act.wait_ge(a_tr, 4 * n + t + 1)
                        act.activation(probT[:, T_OFF[t]:T_OFF[t] + ke], ps[6 + t % 2][:, 0:ke],
                                       ACT.Copy).then_inc(a_trc, 1)

                def body(i, first):
                    for h in range(4):
                        if h % 2 == 0:
                            if not (first and h == 0):
                                probs_T(i, h - 1, first) if h else probs_T(i - 1, 3, False)
                            kq(i, h // 2, first)
                            exps(i, h, first)
                        else:
                            exps(i, h, first)
                            probs_T(i, h - 1, first)
                peeled(act, HEADS // 4, body)
                probs_T(HEADS // 4 - 1, 3, False)

            load(cs[:, 0, :], cT, "c")
            load(kc[:], consts, "const")
            load(xs[:], x.rearrange("(t p) d -> p t d", p=P), "x")
            load(brow[:, 0:6, :], bias_rows[0:1, 0:6 * D].to_broadcast([P, 6 * D]).rearrange("p (r n) -> p r n", r=6), "bias0")
            load(gain[:, 0:2, :], gains[0:1, 0:2 * D].to_broadcast([P, 2 * D]).rearrange("p (r n) -> p r n", r=2), "gain0")
            load(convs[:], conv, "conv")
            load(keyT, keys[0], "keys0")
            load(fw[:], f_w, "fw")
            load(fb[:], f_bias, "fb")
            act.wait_ge(ld["c"], 16)
            act.activation(cs[:, 1, :], cs[:, 0, :], ACT.Exp, scale=-1.0).then_inc(silu_e, 1)
            ada0(C_ADA0, 12, SHIFT)
            ada0(C_ADA0 + 12, 8, F_SHIFT)
            ada0(C_ADA0 + 20, 4, F_GATE0)
            norm("mix0", hT, ld["x"], 16)
            in_proj()
            norm("ffn0", hT, x_mix[0], 4 * N_SQ)
            peer_scores(0, C_PQ0)
            soft(0)
            soft(1)
            gelus(0)
            soft(2)
            gelus(1, with_ada=True)
            soft(3)
            gelus(2)
            gelus(3)
            act.wait_ge(x_ffn[0], NT)
            load(brow, bias_rows[0:1, 6 * D:14 * D].to_broadcast([P, 8 * D]).rearrange("p (r n) -> p r n", r=8), "bias1")
            load(gain, gains[0:1, 2 * D:5 * D].to_broadcast([P, 3 * D]).rearrange("p (r n) -> p r n", r=3), "gain1")
            load(keyT, keys[1], "keys1")
            norm("kv", hT, x_ffn[0], NT)
            forget()
            project_v()
            norm("mix1", hqT, x_ffn[0], NT)
            attention()
            copies("att", hT)
            norm("ffn1", hT, x_mix[1], 4 * N_SQ)
            load(rows[:, SHIFT, :], gains[0:1, 5 * D:6 * D].to_broadcast([P, D]), "gainf")
            peer_scores(1, C_PQ1)
            soft(4)
            soft(5)
            gelus(4)
            soft(6)
            gelus(5)
            soft(7)
            gelus(6)
            gelus(7)
            norm("fin", None, x_ffn[1], NT)

        @block.vector
        def _(dve):
            me = Ticks(dve, dv)

            def silu():
                dve.wait_ge(silu_e, 1)
                me(dve.tensor_scalar(cs[:, 2, :], cs[:, 1, :], 1.0, None, ALU.add))
                me.sync()
                me(dve.reciprocal(cs[:, 1, :], cs[:, 2, :]))
                me.sync()
                me(dve.tensor_tensor(cs[:, 2, :], cs[:, 0, :], cs[:, 1, :], ALU.mult))
                me.sync()
                dve.tensor_copy(sB[:], cs[:, 2, :].unsqueeze(2).to_broadcast([P, KB, P])).then_inc(silu_b, 1)

            def finish_rows(plan):
                for row, b, const, _ in plan:
                    me(dve.scalar_tensor_tensor(rows[:, row, :], rows[:, row, :], const, brow[:, b, :], ALU.add, ALU.add))
                me.sync()
                for row, _, _, g in plan:
                    if g is not None:
                        me(dve.tensor_tensor(rows[:, row, :], rows[:, row, :], gain[:, g, :], ALU.mult))
                me.sync()

            def norm(name, a_row, b_row):
                dve.wait_ge(n_sq[name], NT)
                dve.tensor_scalar(stat[:, 0, :], stat[:, 0, :], 1.0 / D, EPS, ALU.mult, ALU.add).then_inc(n_ms[name], 1)
                dve.wait_ge(n_rt[name], 1)
                me(dve.reciprocal(stat[:, 0, :], stat[:, 1, :]))
                me.sync()
                if name == "fin":
                    dve.wait_ge(ld["gainf"], 16)
                    for t in range(NT):
                        dve.scalar_tensor_tensor(xs[:, t, :], xs[:, t, :], stat[:, 0, t:t + 1], rows[:, SHIFT, :],
                                                 ALU.mult, ALU.mult).then_inc(y_ok, 1)
                    return
                for t in range(NT):
                    me(dve.scalar_tensor_tensor(hs[:, t, :], xs[:, t, :], stat[:, 0, t:t + 1], rows[:, a_row, :],
                                                ALU.mult, ALU.mult))
                    if t:
                        me.sync(1)
                        dve.tensor_tensor(hs[:, t - 1, :], hs[:, t - 1, :], rows[:, b_row, :], ALU.add).then_inc(n_h[name], 1)
                me.sync()
                dve.tensor_tensor(hs[:, NT - 1, :], hs[:, NT - 1, :], rows[:, b_row, :], ALU.add).then_inc(n_h[name], 1)

            def in_proj():
                me(dve.memset(cu[:, :, 0:2], 0.0))
                me.sync()

                def body(i, first):
                    for jp in range(2):
                        J = 4 * i + 2 * jp
                        n = C_IN + 3 * jp
                        me(dve.tensor_copy(taps[:], convs[:, bass.ds(J, 2), :]))
                        w_done(dve, n + 1, 3 * i)
                        for jj in range(2):
                            dve.wait_ge(c_out, J + jj + 1)
                            dve.tensor_tensor(cu[:, jj, 2:2 + S], ps[2 + jj], c_s[:, jj, :], ALU.mult).then_inc(cu_ok, 1)
                        dve.wait_ge(cu_ok, J + 2)
                        me.sync()
                        for jj in range(2):
                            me(dve.tensor_scalar(z_s[:, jj, :], cu[:, jj, 0:S], taps[:, jj, 0:1], None, ALU.mult))
                        for w in (1, 2):
                            for jj in range(2):
                                me.sync(1)
                                me(dve.scalar_tensor_tensor(z_s[:, jj, :], cu[:, jj, w:w + S], taps[:, jj, w:w + 1],
                                                            z_s[:, jj, :], ALU.mult, ALU.add))
                        w_done(dve, n + 2, 3 * i)
                        me.sync()
                        for jj in range(2):
                            dve.tensor_tensor(gT[:, bass.ds(J + jj, 1), :].squeeze(1), ps[4 + jj], z_s[:, jj, :],
                                              ALU.mult).then_inc(g_ok, 1)
                body(0, True)
                body(1, False)

            def add_projection(L, c0, gate_row):
                def body(i, first):
                    for s in range(2):
                        w_done(dve, c0 + s, i)
                        cols = bass.ds((2 * i + s) * CW, CW)
                        done = 2 * NT * i + NT * s
                        if not first:
                            dve.wait_ge(x_mix[L], done - NT)
                        for t in range(NT):
                            dve.tensor_tensor(y_s[:, s, t, :], ps[4 * s + t][:, 0:CW], rows[:, gate_row, cols],
                                              ALU.mult).then_inc(y_in[L], 1)
                        for t in range(NT):
                            dve.wait_ge(y_in[L], done + t + 1)
                            dve.tensor_tensor(xs[:, t, cols], xs[:, t, cols], y_s[:, s, t, :], ALU.add).then_inc(x_mix[L], 1)
                peeled(dve, N_SQ // 2, body)

            def route(T):
                t = T % NT
                with dve.Fori(0, LISTS // 4) as i:
                    me.enter(i, 23)
                    me(dve.tensor_copy(stage, sc[:, t, bass.ds(4 * i, 4), :]))
                    top16([stage[:, l, :] for l in range(4)], tv4, ti4)
                    me(dve.tensor_copy(tv[:, bass.ds(4 * i, 4), :], tv4))
                    me(dve.tensor_copy(tif[:, bass.ds(4 * i, 4), :], ti4))
                    me.sync()
                me.leave(LISTS // 4)
                by_head = tv.rearrange("p (h c) k -> p h c k", c=2)
                idx_by_head = tif.rearrange("p (h c) k -> p h c k", c=2)
                full = [P, 4, TOPK, TOPK]
                pick1 = eq.rearrange("p (n a) -> p n a", a=TOPK)
                pick2 = hf[:, 0:1024].rearrange("p (n a) -> p n a", a=TOPK)
                with dve.Fori(0, 2) as i:
                    me.enter(i, 31)
                    hh = bass.ds(4 * i, 4)
                    me(dve.tensor_tensor(cand, by_head[:, hh, 0, :].unsqueeze(3).to_broadcast(full),
                                         by_head[:, hh, 1, :].unsqueeze(2).to_broadcast(full), ALU.add))
                    top16([candf[:, l, :] for l in range(4)], bv4, bp4.rearrange("p (l k) -> p l k", l=4))
                    me(dve.tensor_copy(bs[:, hh, :], bv4))
                    me(dve.tensor_scalar(ra4, bp4, 4, None, ALU.logical_shift_right))
                    me(dve.tensor_scalar(rb4, bp4, TOPK - 1, None, ALU.bitwise_and))
                    for pick, rank in ((pick1, ra4), (pick2, rb4)):
                        me.sync(0 if pick is pick1 else 1)
                        me(dve.tensor_tensor(pick, iota.unsqueeze(1).to_broadcast([P, 64, TOPK]),
                                             rank.unsqueeze(2).to_broadcast([P, 64, TOPK]), ALU.is_equal))
                    for c, pick in enumerate((pick1, pick2)):
                        me.sync(1)
                        p4 = pick.rearrange("p (h k) a -> p h k a", h=4)
                        me(dve.tensor_tensor(p4, p4, idx_by_head[:, hh, c, :].unsqueeze(2).to_broadcast(full), ALU.mult))
                    for pick, e in ((pick1, e1), (pick2, e2)):
                        me.sync(1)
                        me(dve.tensor_reduce(e, pick, AX_X, ALU.add))
                    me.sync()
                    me(dve.scalar_tensor_tensor(idx[:, T % 2, bass.ds(64 * i, 64)], e1, float(NK), e2, ALU.mult, ALU.add))
                    me.sync()
                me.leave(2)
                dve.tensor_tensor(bd, bs, bs[:, :, 0:1].to_broadcast([P, PH, TOPK]), ALU.subtract).then_inc(r_d, 1)
                dve.wait_ge(r_e, T + 1)
                me(dve.tensor_reduce(gsum[:, 0, :], bd, AX_X, ALU.add))
                me.sync()
                me(dve.reciprocal(gsum[:, 1, :], gsum[:, 0, :]))
                me.sync()
                dve.tensor_tensor(gates[:, T % 2, :].rearrange("p (h k) -> p h k", h=PH), bd,
                                  gsum[:, 1, :].unsqueeze(2).to_broadcast([P, PH, TOPK]), ALU.mult).then_inc(r_ok, 1)

            def top16(lists, best, where):
                def settle():
                    me.sync()
                    dve.nop(nofuse=True)
                for r in range(2):
                    w = slice(8 * r, 8 * r + 8)
                    settle()
                    for l, values in enumerate(lists):
                        me(dve.max(best[:, l, w], values))
                    settle()
                    for l, values in enumerate(lists):
                        me(dve.max_index(where[:, l, w], best[:, l, w], values))
                    if r == 0:
                        settle()
                        for l, values in enumerate(lists):
                            me(dve.match_replace(values, best[:, l, w], values, LOWEST))
                me.sync()

            def experts(T):
                t, base = T % NT, T * (STEPS // 2)
                tok = hs[:, t, :]
                g = gates[:, T % 2, :]
                dve.wait_ge(r_ok, T + 1)
                for b in (6, 7):
                    me(dve.memset(ps[b], 0.0))
                me.sync()

                def dot(n, r):
                    buf = ring[:, HALF * n + r, :]
                    dve.tensor_tensor_reduce(buf, buf, tok, 1.0, 0.0, ALU.mult, ALU.add,
                                             dots[:, n, r:r + 1]).then_inc(u_used[n], 1)

                def weigh(n, f, slot):
                    dve.wait_ge(act_ok[n], f + 1)
                    me(dve.tensor_tensor(coef[:, n, :], acts[:, n, :], g[:, bass.ds(slot, HALF)], ALU.mult))

                def add(n, f, r, first):
                    if r:
                        dve.wait_ge(v_used[n], HALF * f + r)
                    elif not first:
                        dve.wait_ge(v_used[1 - n], HALF * (f + n))
                    dve.scalar_tensor_tensor(acc, ring[:, 8 + HALF * n + r, :], coef[:, n, r:r + 1], acc,
                                             ALU.mult, ALU.add).then_inc(v_used[n], 1)

                def step(nu, fu, nv, fv, slot, first=False):
                    dve.wait_ge(u_got[nu], 16 * HALF * (fu + 1))
                    dot(nu, 0)
                    weigh(nv, fv, slot)
                    dot(nu, 1)
                    dve.wait_ge(v_got[nv], 16 * HALF * (fv + 1))
                    me.sync()
                    add(nv, fv, 0, first)
                    dot(nu, 2)
                    add(nv, fv, 1, first)
                    dot(nu, 3)
                    add(nv, fv, 2, first)
                    add(nv, fv, 3, first)

                dve.wait_ge(u_got[0], 16 * HALF * (base + 1))
                for r in range(HALF):
                    dot(0, r)
                step(1, base, 0, base, 0, first=True)
                step(0, base + 1, 1, base, HALF)
                with dve.Fori(1, STEPS // 2 - 1) as i:
                    me.enter(i - 1, 2)
                    step(1, i + base, 0, i + base, 2 * HALF * i)
                    step(0, i + (base + 1), 1, i + base, 2 * HALF * i + HALF)
                me.leave(STEPS // 2 - 2)
                last = base + STEPS // 2 - 1
                step(1, last, 0, last, SLOTS - 2 * HALF)
                weigh(1, last, SLOTS - HALF)
                dve.wait_ge(v_got[1], 16 * HALF * (last + 1))
                me.sync()
                for r in range(HALF):
                    add(1, last, r, False)
                dve.wait_ge(v_used[1], HALF * (last + 1))
                me(dve.tensor_tensor(eq, acc, rows[:, F_GATE[T // NT], :], ALU.mult))
                me.sync()
                dve.tensor_tensor(xs[:, t, :], xs[:, t, :], eq, ALU.add).then_inc(x_ffn[T // NT], 1)
                dve.wait_ge(x_ffn[T // NT], t + 1)

            def forget():
                me(dve.memset(aux_l, 1.0))
                dve.wait_ge(f_done, 1)
                dve.wait_ge(ld["fb"], 16)
                dve.tensor_scalar(cum, ps[0][0:FR, :], fb[:], None, ALU.add).then_inc(f_z, 1)
                dve.wait_ge(f_l, 1)
                dve.wait_ge(f_z, 1)
                me(dve.scalar_tensor_tensor(aux_b, cum, 0.0, aux_r, ALU.min, ALU.subtract))
                me.sync()
                me(dve.tensor_tensor_scan(cum, aux_l, aux_b, 0.0, ALU.mult, ALU.add))
                me.sync()
                me(dve.tensor_copy(aux_r, cum))
                me(dve.tensor_copy(aux_b, cum))
                me.sync()
                for n in (0, 64):
                    me(dve.memset(aux_b[n:n + 32, :], -1.0))
                    me(dve.memset(aux_r[n + 32:n + 48, :], 1.0))
                me.sync()

            def attention():
                def scores(i, h, first):
                    n = 4 * i + h
                    for t in range(NT):
                        dve.wait_ge(a_s, 4 * n + t + 1)
                        diag = ps[2 + t][:, t * P:(t + 1) * P]
                        me(dve.tensor_tensor(diag, diag, mask, ALU.add))
                        if t:
                            me.sync(1)
                            row_max(h, t - 1)
                    me.sync()
                    row_max(h, NT - 1)

                def row_max(h, t):
                    dve.reduce_max(amax[:, h % 2, t:t + 1], ps[2 + t][:, 0:(t + 1) * P], AX_X,
                                   negate=True).then_inc(a_max, 1)

                def aux(i, h, first):
                    n = 4 * i + h
                    rows48 = slice(64 * (h % 2), 64 * (h % 2) + 48)
                    if not (first and h < 2):
                        dve.wait_ge(a_s, 4 * (n - 1))
                    dve.tensor_tensor(aux_l[rows48, :], aux_b[rows48, :],
                                      kc[rows48, bass.ds(K_SEL + n, 1)].to_broadcast([48, S]), ALU.mult).then_inc(aux_ok, 1)

                def finish(i, h):
                    n = 4 * i + h
                    dve.wait_ge(a_exp, 4 * n + 4)
                    me(dve.reciprocal(ainv[:, h % 2, :], asum[:, h % 2, :]))
                    dve.wait_ge(a_pv, n + 1)
                    me.sync()
                    dve.tensor_tensor(hs[:, :, bass.ds(n * HD, HD)],
                                      ps[h % 2][:, 0:NT * HD].rearrange("p (t d) -> p t d", t=NT),
                                      ainv[:, h % 2, :].unsqueeze(2).to_broadcast([P, NT, HD]), ALU.mult).then_inc(a_o, 1)

                def body(i, first):
                    for h in range(4):
                        aux(i, h, first)
                        if h % 2 == 0:
                            if not (first and h == 0):
                                finish(i, h - 1) if h else finish(i - 1, 3)
                            scores(i, h, first)
                        else:
                            scores(i, h, first)
                            finish(i, h - 1)
                body(0, True)
                with dve.Fori(1, HEADS // 4) as i:
                    me.enter(i - 1, 20)
                    body(i, False)
                me.leave(HEADS // 4 - 1)
                finish(HEADS // 4 - 1, 3)

            dve.wait_ge(ld["c"], 16)
            silu()
            dve.wait_ge(ld["bias0"], 16)
            dve.wait_ge(ld["gain0"], 16)
            dve.wait_ge(ada_out[0], 12)
            finish_rows([(SHIFT, 0, 0.0, None), (SCALE, 1, 1.0, 0), (GATE, 2, 1.0, None)])
            dve.wait_ge(ld["x"], 16)
            norm("mix0", SCALE, SHIFT)
            dve.wait_ge(ada_out[0], N_ADA[0])
            finish_rows([(F_SHIFT, 3, 0.0, None), (F_SCALE, 4, 1.0, 1), (F_GATE0, 5, 1.0, None)])
            dve.wait_ge(ld["conv"], 16)
            in_proj()
            add_projection(0, C_OUT, GATE)
            norm("ffn0", F_SCALE, F_SHIFT)
            dve.wait_ge(s_out[0], LISTS)
            dve.wait_ge(ld["const"], 16)
            route(0)
            route(1)
            experts(0)
            route(2)
            experts(1)
            route(3)
            experts(2)
            experts(3)
            dve.wait_ge(ld["bias1"], 16)
            dve.wait_ge(ld["gain1"], 16)
            dve.wait_ge(ada_out[1], N_ADA[1])
            finish_rows([(SHIFT, 0, 0.0, None), (SCALE, 1, 1.0, 1), (GATE, 2, 1.0, None),
                         (KV_SHIFT, 3, 0.0, None), (KV_SCALE, 4, 1.0, 0),
                         (F_SHIFT, 5, 0.0, None), (F_SCALE, 6, 1.0, 2), (F_GATE1, 7, 1.0, None)])
            norm("kv", KV_SCALE, KV_SHIFT)
            forget()
            norm("mix1", SCALE, SHIFT)
            attention()
            add_projection(1, C_WO, GATE)
            norm("ffn1", F_SCALE, F_SHIFT)
            dve.wait_ge(s_out[1], LISTS)
            route(4)
            route(5)
            experts(4)
            route(6)
            experts(5)
            route(7)
            experts(6)
            experts(7)
            norm("fin", None, None)

        @block.gpsimd
        def _(pool):
            def gather(kind, T, n, f, slot, first=False):
                table, at, ids, got, used, copied = (
                    (tables[2 * (T // NT)], 0, idx_u, u_got, u_used, ix_u) if kind == "u" else
                    (tables[2 * (T // NT) + 1], 8, idx_v, v_got, v_used, ix_v))
                if not first:
                    pool.wait_ge(used[n], HALF * f)
                    pool.nop(nofuse=True)
                pool.tensor_copy(ids[:, n, :], idx[:, T % 2, bass.ds(slot, HALF)]).then_inc(copied, 1)
                pool.wait_ge(copied, 2 * f + (n + 1))
                pool.nop(nofuse=True)
                for r in range(HALF):
                    pool.indirect_dma_start(ring[:, at + HALF * n + r, :], None, table,
                                            bass.IndirectOffsetOnAxis(ap=ids[:, n, r:r + 1], axis=0)).then_inc(got[n], 16)

            def tile(T):
                base = T * (STEPS // 2)
                new = T == 0
                pool.wait_ge(r_ok, T + 1)
                gather("u", T, 0, base, 0, new)
                gather("u", T, 1, base, HALF, new)
                gather("v", T, 0, base, 0, new)
                gather("u", T, 0, base + 1, 2 * HALF)
                gather("v", T, 1, base, HALF, new)
                with pool.Fori(1, STEPS // 2 - 1) as i:
                    gather("u", T, 1, i + base, 2 * HALF * i + HALF)
                    gather("v", T, 0, i + base, 2 * HALF * i)
                    gather("u", T, 0, i + (base + 1), 2 * HALF * i + 2 * HALF)
                    gather("v", T, 1, i + base, 2 * HALF * i + HALF)
                last = base + STEPS // 2 - 1
                gather("u", T, 1, last, SLOTS - HALF)
                gather("v", T, 0, last, SLOTS - 2 * HALF)
                gather("v", T, 1, last, SLOTS - HALF)

            for T in range(2 * NT):
                tile(T)


INPUTS = ["x", "cT", "consts", "conv", "f_w", "f_bias", "bias_rows", "gains", "keys", "wstream",
          "u0", "v0", "u1", "v1"]


def kernel(**inputs):
    import numpy as np
    import concourse.bacc as bacc
    from concourse.bass_utils import run_bass_kernel_spmd as run

    a = {k: np.asarray(v) for k, v in inputs.items()}

    def chunks(w):
        return w.reshape(KB, P, -1, CW).transpose(2, 1, 0, 3).reshape(-1, P, KB * CW)

    w_in = a["a_w_in"][0].reshape(D, 3, N_SQ, CW)[:, [1, 2, 0]].transpose(0, 2, 1, 3).reshape(D, 3 * D)
    w_k, w_v, w_f = a["kv_w"][:, 0:D], a["kv_w"][:, D:2 * D], a["kv_w"][:, 2 * D:]
    w_kq = np.stack([w_k.reshape(D, KB, P), a["b_w_q"][0].reshape(D, KB, P)], axis=2).reshape(D, 2 * D)
    stream = [a["mix_ada_w"][0], a["ffn_ada_w"][0], w_in, a["a_w_out"][0], a["peer_w_q"][0],
              a["mix_ada_w"][1], a["kv_ada_w"], a["ffn_ada_w"][1], w_v, w_kq, a["b_w_o"][0], a["peer_w_q"][1]]
    consts = np.zeros((P, K_COLS), np.float32)
    consts[:, K_ID:K_ID + P] = np.eye(P)
    consts[:, K_MASK:K_MASK + P] = np.where(np.arange(P)[None, :] <= np.arange(P)[:, None], 0.0, -1.0e30)
    consts[:, K_IOTA:K_IOTA + TOPK] = np.arange(TOPK)
    for n in (0, 32, 64, 96):
        consts[n:n + HEADS, K_SEL:K_SEL + HEADS] = np.eye(HEADS)
    consts[:, K_ONE] = 1.0
    arrays = {
        "x": a["x"][0],
        "cT": a["c"].reshape(KB, P).T,
        "consts": consts,
        "conv": a["a_conv"][0].reshape(3, KB, P).transpose(2, 1, 0),
        "f_w": np.tile(w_f.reshape(KB, P, HEADS).transpose(1, 0, 2), (1, 1, FR // HEADS)),
        "f_bias": np.tile(a["f_bias"].reshape(HEADS, 1), (FR // HEADS, 1)),
        "bias_rows": np.concatenate([a["mix_ada_b"][0], a["ffn_ada_b"][0], a["mix_ada_b"][1], a["kv_ada_b"],
                                     a["ffn_ada_b"][1]]).reshape(1, -1),
        "gains": np.concatenate([a["mix_norm"][0], a["ffn_norm"][0], a["kv_norm"], a["mix_norm"][1],
                                 a["ffn_norm"][1], a["final_norm"]]).reshape(1, -1),
        "keys": a["peer_sub_keys"].reshape(2, LISTS * NK, DK).transpose(0, 2, 1),
        "wstream": np.concatenate([chunks(w) for w in stream]),
        "u0": a["peer_u"][0], "v0": a["peer_v"][0], "u1": a["peer_u"][1], "v1": a["peer_v"][1],
    }
    nc = bacc.Bacc("TRN2", target_bir_lowering=False, num_devices=1)
    arrays = {f"in_{k}": np.ascontiguousarray(arrays[k]) for k in INPUTS}
    aps = [nc.dram_tensor(k, v.shape, mybir.dt.from_np(v.dtype), kind="ExternalInput").ap() for k, v in arrays.items()]
    out = nc.dram_tensor("out_y", (S, D), F32, kind="ExternalOutput").ap()
    bass_trunk(nc, *aps[:10], aps[10:], out)
    r = run(nc, [arrays], core_ids=[0])
    return r.results[0]["out_y"].reshape(1, S, D)
```

```python
from contextlib import ExitStack

import concourse.bass as bass
from concourse import mybir

ALU = mybir.AluOpType
ACT = mybir.ActivationFunctionType
F32 = mybir.dt.float32
U32 = mybir.dt.uint32
AX_X = mybir.AxisListType.X

P = 128
D = 1024
S = 512
NT = S // P
KB = D // P
HEADS = 16
HD = D // HEADS
PH = 8
NK = 128
DK = 128
TOPK = 16
LISTS = 2 * PH
SLOTS = PH * TOPK
CW = 256
EPS = 1e-6
LOWEST = -3.0e38
FR = 112

N_ADA = (6 * D // CW, 8 * D // CW)
N_IN = 3 * D // CW
N_SQ = D // CW
N_PQ = 2 * D // CW
N_KQ = 2 * D // CW
C_ADA0 = 0
C_IN = C_ADA0 + N_ADA[0]
C_OUT = C_IN + N_IN
C_PQ0 = C_OUT + N_SQ
C_ADA1 = C_PQ0 + N_PQ
C_V = C_ADA1 + N_ADA[1]
C_KQ = C_V + N_SQ
C_WO = C_KQ + N_KQ
C_PQ1 = C_WO + N_SQ
N_CHUNKS = C_PQ1 + N_PQ

SHIFT, SCALE, GATE, KV_SHIFT, KV_SCALE, F_SHIFT, F_SCALE, F_GATE1, F_GATE0 = range(9)
F_GATE = (F_GATE0, F_GATE1)

K_ID, K_MASK, K_IOTA, K_SEL, K_ONE = 0, 128, 256, 272, 288
K_COLS = 289

HALF = 4
BY_PE = 2
BY_DVE = HALF - BY_PE
STEPS = SLOTS // HALF


class Ticks:

    def __init__(self, eng, sem):
        self.eng, self.sem, self.n, self.turn, self.per, self.start = eng, sem, 0, None, 0, 0

    def __call__(self, ins):
        ins.then_inc(self.sem, 1)
        self.n += 1

    def sync(self, back=0):
        n = self.n - back
        self.eng.wait_ge(self.sem, n if self.turn is None else self.turn * self.per + n)

    def enter(self, turn, per):
        self.turn, self.per, self.start = turn, per, self.n

    def leave(self, times):
        assert self.n - self.start == self.per, (self.n - self.start, self.per)
        self.n = self.start + self.per * times
        self.turn = None


def peeled(eng, times, body):
    body(0, True)
    if times > 1:
        with eng.Fori(1, times) as i:
            body(i, False)


def window(eng, turn, segments, ticks=None):
    at = 1
    for n, times, work, steps in segments:
        with eng.Fori(0, times) as k:
            if ticks:
                ticks.enter(k, steps)
            for c in range(n):
                turn(n * k + (at + c))
            if work:
                work(k)
        if ticks:
            ticks.leave(times)
        at += n * times
    assert at == STEPS // 2 - 1


def bass_trunk(nc, x, cT, consts, conv, f_w, f_bias, bias_rows, gains, keys, wstream, tables, out):
    with ExitStack() as ctx:
        def sb(name, shape, dt=F32):
            return ctx.enter_context(nc.sbuf_tensor(name, shape, dt))

        def sem(name):
            return ctx.enter_context(nc.semaphore(name))

        xs = sb("xs", [P, NT, D])
        hs = sb("hs", [P, NT, D])
        hT = sb("hT", [P, KB, S])
        rows = sb("rows", [P, 9, D])
        ring = sb("ring", [P, 16, D])
        wring = sb("wring", [P, 2, KB, CW])
        sc = sb("sc", [P, NT, LISTS, NK])
        kc = sb("kc", [P, K_COLS])
        cs = sb("cs", [P, 3, KB])
        sB = sb("sB", [P, KB, P])
        convs = sb("convs", [P, KB, 3])
        taps = sb("taps", [P, 2, 3])
        stat = sb("stat", [P, 2, NT])
        fb = sb("fb", [FR, 1])
        idx = sb("idx", [P, 2, SLOTS], U32)
        gates = sb("gates", [P, 2, SLOTS])
        gsum = sb("gsum", [P, 2, PH])
        idx_u = sb("idx_u", [P, 2, HALF], U32)
        idx_v = sb("idx_v", [P, 2, HALF], U32)
        dots = sb("dots", [P, 2, HALF])
        acts = sb("acts", [P, 2, HALF])
        coef = sb("coef", [P, 2, HALF])
        diag = sb("diag", [P, 2, BY_PE, P])
        amax = sb("amax", [P, 2, NT])
        asum = sb("asum", [P, 2, NT])
        ainv = sb("ainv", [P, 2, NT])
        psum = ctx.enter_context(nc.psum_tensor("psum", [P, 8, 512], F32))
        ps = [psum[:, b, :] for b in range(8)]
        acc = psum[:, 6:8, :].rearrange("p a b -> p (a b)")
        acc_pe = psum[:, 4:6, :].rearrange("p a b -> p (a b)")

        ident = kc[:, K_ID:K_ID + P]
        mask = kc[:, K_MASK:K_MASK + P]
        iota = kc[:, K_IOTA:K_IOTA + TOPK]
        one = kc[:, K_ONE:K_ONE + 1]

        brow = ring[:, 0:8, :]
        gain = ring[:, 8:11, :]
        fw = ring[:, 13, 0:KB * FR].rearrange("p (k n) -> p k n", k=KB)
        keyT = ring[:, 14:16, :].rearrange("p a b -> p (a b)")
        c_s = ring[:, 10, :].rearrange("p (j t) -> p j t", j=2)
        cu = ring[:, 11:13, :].rearrange("p a b -> p (a b)")[:, 0:2 * (S + 2)].rearrange("p (j t) -> p j t", j=2)
        z_s = ring[:, 13, :].rearrange("p (j t) -> p j t", j=2)
        y_s = ring[:, 12:14, :].rearrange("p s (t n) -> p s t n", t=NT)
        qs = ring[:, 1, :].rearrange("p (j t) -> p j t", j=2)
        gT = hs[:].rearrange("p t n -> p (t n)").rearrange("p (k t) -> p k t", k=KB)
        hqT = ring[:, 0:4, :].rearrange("p a b -> p (a b)").rearrange("p (k t) -> p k t", k=KB)
        vs = ring[:, 4:8, :]
        kqs = ring[:, 11:13, :].rearrange("p a (b t) -> p a b t", b=2)

        scf = sc[:].rearrange("p a b c -> p (a b c)")
        cum = scf[0:FR, 0:512]
        aux_r = scf[0:FR, 512:1024]
        aux_b = scf[0:FR, 1024:1536]
        aux_l = scf[0:FR, 1536:2048]
        T_OFF = [0, 128, 384, 768]
        prob = scf[:, 2560:5120].rearrange("p (a b) -> p a b", a=2)
        probT = scf[:, 5120:6400]

        hf = hT[:].rearrange("p a b -> p (a b)")
        cand = hf[:, 0:1024].rearrange("p (h a b) -> p h a b", h=4, a=TOPK)
        candf = hf[:, 0:1024].rearrange("p (h c) -> p h c", h=4)
        eq = hf[:, 1024:2048]
        stage = hf[:, 1024:1536].rearrange("p (l k) -> p l k", l=4)
        tv = hf[:, 2048:2304].rearrange("p (l k) -> p l k", l=LISTS)
        tif = hf[:, 2304:2560].rearrange("p (l k) -> p l k", l=LISTS)
        tv4 = hf[:, 2560:2624].rearrange("p (l k) -> p l k", l=4)
        ti4 = hf[:, 2624:2688].rearrange("p (l k) -> p l k", l=4).bitcast(U32)
        bv4 = hf[:, 2688:2752].rearrange("p (l k) -> p l k", l=4)
        bp4 = hf[:, 2752:2816].bitcast(U32)
        ra4 = hf[:, 2816:2880].bitcast(U32)
        rb4 = hf[:, 2880:2944].bitcast(U32)
        e1 = hf[:, 2944:3008]
        e2 = hf[:, 3008:3072]
        bs = hf[:, 3072:3200].rearrange("p (h k) -> p h k", h=PH)
        bd = hf[:, 3200:3328].rearrange("p (h k) -> p h k", h=PH)

        names = ("x c const conv fw fb bias0 gain0 keys0 bias1 gain1 keys1 gainf").split()
        ld = {n: sem("ld_" + n) for n in names}
        w_got = [sem(f"w_got{s}") for s in range(2)]
        w_used = [sem(f"w_used{s}") for s in range(2)]
        dv, av = sem("dv"), sem("av")
        silu_e, silu_b = sem("silu_e"), sem("silu_b")
        ada_out = [sem(f"ada_out{i}") for i in range(2)]
        rows_ok = [sem(f"rows_ok{i}") for i in range(2)]
        x_mix = [sem(f"x_mix{i}") for i in range(2)]
        x_ffn = [sem(f"x_ffn{i}") for i in range(2)]
        NORMS = ["mix0", "ffn0", "kv", "mix1", "ffn1", "fin"]
        n_sq = {n: sem(f"sumsq_{n}") for n in NORMS}
        n_ms = {n: sem(f"meansq_{n}") for n in NORMS}
        n_rt = {n: sem(f"root_{n}") for n in NORMS}
        n_h = {n: sem(f"h_{n}") for n in NORMS}
        n_tr = {n: sem(f"tr_{n}") for n in NORMS + ["att"]}
        n_hT = {n: sem(f"hT_{n}") for n in NORMS + ["att"]}
        c_out, cu_ok, g_ok = sem("c_out"), sem("cu_ok"), sem("g_ok")
        y_in = [sem(f"y_in{i}") for i in range(2)]
        q_out = [sem(f"q_out{i}") for i in range(2)]
        s_done = [sem(f"s_done{i}") for i in range(2)]
        s_out = [sem(f"s_out{i}") for i in range(2)]
        f_done, f_z, f_l = sem("f_done"), sem("f_z"), sem("f_l")
        v_out = sem("v_out")
        k_out = sem("k_out")
        aux_ok, a_s, a_max, a_exp = sem("aux_ok"), sem("a_s"), sem("a_max"), sem("a_exp")
        a_tr, a_trc, a_pv, a_o = sem("a_tr"), sem("a_trc"), sem("a_pv"), sem("a_o")
        r_d, r_e, r_ok = sem("r_d"), sem("r_e"), sem("r_ok")
        u_got = [sem(f"u_got{n}") for n in range(2)]
        v_got = [sem(f"v_got{n}") for n in range(2)]
        u_used = [sem(f"u_used{n}") for n in range(2)]
        v_used = [sem(f"v_used{n}") for n in range(2)]
        v_used_pe = [sem(f"v_used_pe{n}") for n in range(2)]
        coef_ok = [sem(f"coef_ok{n}") for n in range(2)]
        diag_ok = [sem(f"diag_ok{n}") for n in range(2)]
        ix_u, ix_v = sem("ix_u"), sem("ix_v")
        act_ok = [sem(f"act_ok{n}") for n in range(2)]
        y_ok, stored, cu_0 = sem("y_ok"), sem("stored"), sem("cu_0")

        block = ctx.enter_context(nc.Block())

        def w_ready(eng, n, i=0):
            eng.wait_ge(w_got[n % 2], 16 * (n // 2 + 1) + 16 * i)

        def w_done(eng, n, i=0):
            eng.wait_ge(w_used[n % 2], n // 2 + 1 + i)

        @block.sync
        def _(sp):
            def chunks(i, first):
                for s in range(2):
                    if not first:
                        sp.wait_ge(w_used[s], i)
                    sp.dma_start(wring[:, s].rearrange("p k n -> p (k n)"),
                                 wstream[2 * i + s]).then_inc(w_got[s], 16)
            peeled(sp, N_CHUNKS // 2, chunks)
            sp.wait_ge(y_ok, NT)
            sp.dma_start(out.rearrange("(t p) d -> p t d", p=P), xs[:]).then_inc(stored, 16)
            sp.wait_ge(stored, 16)

        @block.tensor
        def _(pe):
            def ada_pair(which, pair, i=0):
                for s in range(2):
                    w_ready(pe, (C_ADA0, C_ADA1)[which] + 2 * pair + s, i)
                    if pair:
                        pe.wait_ge(ada_out[which], 2 * i + (2 * pair - 1 + s))
                    for k in range(KB):
                        mm = pe.matmul(ps[s][:, 0:CW], sB[:, k, :], wring[:, s, k, :],
                                       start=(k == 0), stop=(k == KB - 1))
                    mm.then_inc(w_used[s], 1)

            def transposes(name, src, ready):
                for t in range(NT):
                    ready(t)
                    for half in range(2):
                        b = 4 + 2 * (t % 2) + half
                        if t >= 2:
                            pe.wait_ge(n_hT[name], 2 * (t - 2) + half + 1)
                        for j in range(4):
                            k = 4 * half + j
                            mm = pe.transpose(ps[b][:, j * P:(j + 1) * P], src[:, t, k * P:(k + 1) * P], ident)
                        mm.then_inc(n_tr[name], 1)

            def norm_T(name):
                transposes(name, hs, lambda t: pe.wait_ge(n_h[name], t + 1))

            def in_proj():
                pe.wait_ge(n_hT["mix0"], 2 * NT)
                pe.wait_ge(ada_out[0], N_ADA[0])

                def body(i, first):
                    for jp in range(2):
                        for third in range(3):
                            n = C_IN + 3 * jp + third
                            w_ready(pe, n, 3 * i)
                            if not (first and jp == 0):
                                s_free = (c_out, cu_ok, g_ok)[third]
                                pe.wait_ge(s_free, 4 * i + 2 * jp)
                            for jj in range(2):
                                for k in range(KB):
                                    mm = pe.matmul(ps[2 * third + jj], wring[:, n % 2, k, jj * P:(jj + 1) * P],
                                                   hT[:, k, :], start=(k == 0), stop=(k == KB - 1))
                            mm.then_inc(w_used[n % 2], 1)
                peeled(pe, 2, body)

            def project(src, c0, free):
                def body(i, first):
                    for s in range(2):
                        w_ready(pe, c0 + s, i)
                        for t in range(NT):
                            if not first:
                                pe.wait_ge(free, 4 * (2 * i + s - 2) + t + 1)
                            for k in range(KB):
                                mm = pe.matmul(ps[4 * s + t][:, 0:CW], src[:, k, t * P:(t + 1) * P],
                                               wring[:, s, k, :], start=(k == 0), stop=(k == KB - 1))
                        mm.then_inc(w_used[s], 1)
                peeled(pe, N_SQ // 2, body)

            def peer_scores(L, c0):
                name = f"ffn{L}"
                pe.wait_ge(n_hT[name], 2 * NT)
                pe.wait_ge(ld[f"keys{L}"], 16)

                def body(i, first):
                    for s in range(2):
                        w_ready(pe, c0 + s, i)
                        n2 = 2 * s
                        for b in range(2):
                            if not (first and s == 0):
                                pe.wait_ge(q_out[L], 4 * i + n2 - 1 + b)
                            for k in range(KB):
                                mm = pe.matmul(ps[b], wring[:, s, k, b * P:(b + 1) * P], hT[:, k, :],
                                               start=(k == 0), stop=(k == KB - 1))
                        mm.then_inc(w_used[s], 1)
                        for b in range(2):
                            pe.wait_ge(q_out[L], 4 * i + n2 + b + 1)
                            if not (first and s == 0):
                                pe.wait_ge(s_out[L], 4 * i + n2 - 1 + b)
                            for t in range(NT):
                                mm = pe.matmul(ps[2 + b][:, t * P:(t + 1) * P], qs[:, b, t * P:(t + 1) * P],
                                               keyT[:, bass.ds((4 * i + n2 + b) * NK, NK)], start=True, stop=True)
                            mm.then_inc(s_done[L], 1)
                peeled(pe, N_PQ // 2, body)

            def forget():
                pe.wait_ge(n_hT["kv"], 2 * NT)
                pe.wait_ge(ld["fw"], 16)
                pe.wait_ge(ada_out[1], N_ADA[1])
                for k in range(KB):
                    mm = pe.matmul(ps[0][0:FR, :], fw[:, k, :], hT[:, k, :], start=(k == 0), stop=(k == KB - 1))
                mm.then_inc(f_done, 1)

            def attention():
                pe.wait_ge(n_hT["mix1"], 2 * NT)
                pe.wait_ge(v_out, 4 * N_SQ)

                def kq(i, s, first):
                    w_ready(pe, C_KQ + s, i)
                    if not (first and s == 0):
                        pe.wait_ge(a_o, 4 * i + 2 * s - 1)
                    for k in range(KB):
                        pe.matmul(ps[0], wring[:, s, k, 0:P], hT[:, k, :], start=(k == 0), stop=(k == KB - 1))
                    if not (first and s == 0):
                        pe.wait_ge(a_o, 4 * i + 2 * s)
                    for k in range(KB):
                        mm = pe.matmul(ps[1], wring[:, s, k, P:2 * P], hqT[:, k, :],
                                       start=(k == 0), stop=(k == KB - 1))
                    mm.then_inc(w_used[s], 1)

                def scores(i, h, first):
                    s, hh = h // 2, h % 2
                    pb = 64 * hh
                    if hh == 0:
                        pe.wait_ge(k_out, 4 * i + 2 * s + 2)
                    pe.wait_ge(aux_ok, 4 * i + h + 1)
                    for t in range(NT):
                        if not (first and h == 0):
                            pe.wait_ge(a_exp, 4 * (4 * i + h - 1) + t + 1)
                        ke = (t + 1) * P
                        pe.matmul(ps[2 + t][:, 0:ke], kqs[pb:pb + 64, s, 1, t * P:ke], kqs[pb:pb + 64, s, 0, 0:ke],
                                  start=True, stop=False)
                        pe.matmul(ps[2 + t][:, 0:ke], aux_l[pb:pb + 48, t * P:ke], aux_r[pb:pb + 48, 0:ke],
                                  start=False, stop=True).then_inc(a_s, 1)

                def values(i, h, first):
                    n = 4 * i + h
                    for t in range(NT):
                        pe.wait_ge(a_exp, 4 * n + t + 1)
                        if not (first and h == 0 and t < 2):
                            pe.wait_ge(a_trc, 4 * n + t - 1)
                        for kb in range(t + 1):
                            mm = pe.transpose(ps[6 + t % 2][:, kb * P:(kb + 1) * P],
                                              prob[:, h % 2, T_OFF[t] + kb * P:T_OFF[t] + (kb + 1) * P], ident)
                        mm.then_inc(a_tr, 1)
                    if not (first and h < 2):
                        pe.wait_ge(a_o, n - 1)
                    for t in range(NT):
                        pe.wait_ge(a_trc, 4 * n + t + 1)
                        for kb in range(t + 1):
                            mm = pe.matmul(ps[h % 2][:, t * HD:(t + 1) * HD],
                                           probT[:, T_OFF[t] + kb * P:T_OFF[t] + (kb + 1) * P],
                                           vs[:, kb, bass.ds(n * HD, HD)], start=(kb == 0), stop=(kb == t))
                    mm.then_inc(a_pv, 1)

                def body(i, first):
                    for h in range(4):
                        if h % 2 == 0:
                            if not (first and h == 0):
                                values(i, h - 1, first) if h else values(i - 1, 3, False)
                            kq(i, h // 2, first)
                            scores(i, h, first)
                        else:
                            scores(i, h, first)
                            values(i, h - 1, first)
                peeled(pe, HEADS // 4, body)
                values(HEADS // 4 - 1, 3, False)

            def add_rows(T, segments):
                base = T * (STEPS // 2)

                def half(n, f, start=False, stop=False):
                    pe.wait_ge(v_got[n], 16 * HALF * (f + 1))
                    pe.wait_ge(diag_ok[n], BY_PE * (f + 1))
                    for j in range(BY_PE):
                        for c in range(2):
                            mm = pe.matmul(ps[4 + c], diag[:, n, j, :],
                                           ring[:, 8 + HALF * n + BY_DVE + j, c * 512:(c + 1) * 512],
                                           start=start and j == 0, stop=stop and j == BY_PE - 1,
                                           skip_group_check=True)
                    mm.then_inc(v_used_pe[n], 1)

                def turn(i):
                    half(0, i + base)
                    half(1, i + base)
                if T % NT:
                    pe.wait_ge(x_ffn[T // NT], T % NT)
                half(0, base, start=True)
                half(1, base)
                window(pe, turn, segments)
                end = base + STEPS // 2 - 1
                half(0, end)
                half(1, end, stop=True)

            pe.wait_ge(silu_b, 1)
            ada_pair(0, 0)
            with pe.Fori(0, N_ADA[0] // 2 - 1) as i:
                ada_pair(0, 1, i)
            pe.wait_ge(ld["const"], 16)
            norm_T("mix0")
            in_proj()
            pe.wait_ge(g_ok, KB)
            project(gT, C_OUT, y_in[0])
            pe.wait_ge(y_in[0], 4 * N_SQ)
            norm_T("ffn0")
            peer_scores(0, C_PQ0)
            pe.wait_ge(s_out[0], LISTS)
            plain = [(1, STEPS // 2 - 2, None, 0)]
            add_rows(0, plain)
            ada_pair(1, 0)
            add_rows(1, [(1, 14, lambda k: ada_pair(1, 1, k), 0)])
            add_rows(2, [(1, 1, lambda k: ada_pair(1, 15, k), 0), (1, 13, None, 0)])
            add_rows(3, plain)
            norm_T("kv")
            forget()
            pe.wait_ge(f_z, 1)
            project(hT, C_V, v_out)
            norm_T("mix1")
            attention()
            pe.wait_ge(a_o, HEADS)
            transposes("att", hs, lambda t: None)
            pe.wait_ge(n_hT["att"], 2 * NT)
            project(hT, C_WO, y_in[1])
            pe.wait_ge(y_in[1], 4 * N_SQ)
            norm_T("ffn1")
            peer_scores(1, C_PQ1)
            pe.wait_ge(s_out[1], LISTS)
            for T in range(NT, 2 * NT):
                add_rows(T, plain)

        @block.scalar
        def _(act):
            def load(dst, src, name):
                act.dma_start(dst, src).then_inc(ld[name], 16)

            me = Ticks(act, av)

            flat_rows = rows[:].rearrange("p r n -> p (r n)")

            def ada_pair(which, c0, row0, i):
                for s in range(2):
                    w_done(act, c0 + s, i)
                    act.activation(flat_rows[:, bass.ds(row0 * D + (2 * i + s) * CW, CW)], ps[s][:, 0:CW],
                                   ACT.Copy).then_inc(ada_out[which], 1)

            def ada0(c0, n, row0):
                with act.Fori(0, n // 2) as i:
                    ada_pair(0, c0, row0, i)

            def copies(name, dst):
                for t in range(NT):
                    for half in range(2):
                        b = 4 + 2 * (t % 2) + half
                        act.wait_ge(n_tr[name], 2 * t + half + 1)
                        act.activation(dst[:, 4 * half:4 * half + 4, t * P:(t + 1) * P],
                                       ps[b].rearrange("p (j t) -> p j t", j=4), ACT.Copy).then_inc(n_hT[name], 1)

            def norm(name, dst, x_sem, x_count):
                act.wait_ge(x_sem, x_count)
                for t in range(NT):
                    act.activation(hs[:, t, :], xs[:, t, :], ACT.Square,
                                   accum_out=stat[:, 0, t:t + 1]).then_inc(n_sq[name], 1)
                act.wait_ge(n_ms[name], 1)
                act.activation(stat[:, 1, :], stat[:, 0, :], ACT.Sqrt).then_inc(n_rt[name], 1)
                if dst is not None:
                    copies(name, dst)

            def in_proj():
                def body(i, first):
                    for jp in range(2):
                        n = C_IN + 3 * jp
                        w_done(act, n, 3 * i)
                        if not (first and jp == 0):
                            act.wait_ge(cu_ok, 4 * i + 2 * jp)
                        for jj in range(2):
                            act.activation(c_s[:, jj, :], ps[jj], ACT.Copy).then_inc(c_out, 1)
                peeled(act, 2, body)

            def peer_scores(L, c0):
                def body(i, first):
                    for s in range(2):
                        w_done(act, c0 + s, i)
                        for b in range(2):
                            if not (first and s == 0):
                                act.wait_ge(s_done[L], 4 * i + 2 * s - 1 + b)
                            act.activation(qs[:, b, :], ps[b], ACT.Copy).then_inc(q_out[L], 1)
                        for b in range(2):
                            act.wait_ge(s_done[L], 4 * i + 2 * s + b + 1)
                            act.activation(sc[:, :, 4 * i + 2 * s + b, :], ps[2 + b].rearrange("p (t k) -> p t k", t=NT),
                                           ACT.Copy).then_inc(s_out[L], 1)
                peeled(act, N_PQ // 2, body)

            def soft(T):
                act.wait_ge(r_d, T + 1)
                act.activation(bd, bd, ACT.Exp).then_inc(r_e, 1)

            def gelus(T, segments, last=None):
                base = T * (STEPS // 2)

                def half(n, f):
                    act.wait_ge(u_used[n], HALF * (f + 1))
                    act.activation(acts[:, n, :], dots[:, n, :], ACT.Gelu_apprx_tanh).then_inc(act_ok[n], 1)

                def spread(n, f, new=False):
                    act.wait_ge(coef_ok[n], f + 1)
                    if not new:
                        act.wait_ge(v_used_pe[n], f)
                    for j in range(BY_PE):
                        act.activation(diag[:, n, j, :], ident, ACT.Copy,
                                       scale=coef[:, n, BY_DVE + j:BY_DVE + j + 1]).then_inc(diag_ok[n], 1)

                def turn(i, new=False):
                    spread(0, i + base, new)
                    half(1, i + base)
                    spread(1, i + base, new)
                    half(0, i + (base + 1))
                half(0, base)
                turn(0, T == 0)
                window(act, turn, segments)
                if last:
                    last()
                end = base + STEPS // 2 - 1
                spread(0, end)
                half(1, end)
                spread(1, end)

            def forget():
                act.wait_ge(f_z, 1)
                me(act.activation(aux_r, cum, ACT.Abs))
                me.sync()
                me(act.activation(aux_b, aux_r, ACT.Exp, scale=-1.0))
                me.sync()
                act.activation(aux_r, aux_b, ACT.Ln, bias=one[0:FR, :]).then_inc(f_l, 1)

            def project_v():
                def body(i, first):
                    for s in range(2):
                        w_done(act, C_V + s, i)
                        for t in range(NT):
                            act.activation(vs[:, t, bass.ds((2 * i + s) * CW, CW)], ps[4 * s + t][:, 0:CW],
                                           ACT.Copy).then_inc(v_out, 1)
                peeled(act, N_SQ // 2, body)

            def attention():
                def kq(i, s, first):
                    w_done(act, C_KQ + s, i)
                    if not first:
                        act.wait_ge(a_s, 16 * i + 8 * s - 8)
                    act.activation(kqs[:, s, 0, :], ps[0], ACT.Copy).then_inc(k_out, 1)
                    act.activation(kqs[:, s, 1, :], ps[1], ACT.Copy, scale=HD ** -0.5).then_inc(k_out, 1)

                def exps(i, h, first):
                    n = 4 * i + h
                    if not (first and h < 2):
                        act.wait_ge(a_tr, 4 * (n - 1))
                    for t in range(NT):
                        ke = (t + 1) * P
                        act.wait_ge(a_max, 4 * n + t + 1)
                        act.activation(prob[:, h % 2, T_OFF[t]:T_OFF[t] + ke], ps[2 + t][:, 0:ke], ACT.Exp,
                                       bias=amax[:, h % 2, t:t + 1],
                                       accum_out=asum[:, h % 2, t:t + 1]).then_inc(a_exp, 1)

                def probs_T(i, h, first):
                    n = 4 * i + h
                    if not (first and h == 0):
                        act.wait_ge(a_pv, n)
                    for t in range(NT):
                        ke = (t + 1) * P
                        act.wait_ge(a_tr, 4 * n + t + 1)
                        act.activation(probT[:, T_OFF[t]:T_OFF[t] + ke], ps[6 + t % 2][:, 0:ke],
                                       ACT.Copy).then_inc(a_trc, 1)

                def body(i, first):
                    for h in range(4):
                        if h % 2 == 0:
                            if not (first and h == 0):
                                probs_T(i, h - 1, first) if h else probs_T(i - 1, 3, False)
                            kq(i, h // 2, first)
                            exps(i, h, first)
                        else:
                            exps(i, h, first)
                            probs_T(i, h - 1, first)
                peeled(act, HEADS // 4, body)
                probs_T(HEADS // 4 - 1, 3, False)

            load(cs[:, 0, :], cT, "c")
            load(kc[:], consts, "const")
            load(xs[:], x.rearrange("(t p) d -> p t d", p=P), "x")
            load(brow[:, 0:6, :], bias_rows[0:1, 0:6 * D].to_broadcast([P, 6 * D]).rearrange("p (r n) -> p r n", r=6), "bias0")
            load(gain[:, 0:2, :], gains[0:1, 0:2 * D].to_broadcast([P, 2 * D]).rearrange("p (r n) -> p r n", r=2), "gain0")
            load(convs[:], conv, "conv")
            load(keyT, keys[0], "keys0")
            load(fb[:], f_bias, "fb")
            act.wait_ge(ld["c"], 16)
            act.activation(cs[:, 1, :], cs[:, 0, :], ACT.Exp, scale=-1.0).then_inc(silu_e, 1)
            ada0(C_ADA0, 12, SHIFT)
            ada0(C_ADA0 + 12, 8, F_SHIFT)
            ada0(C_ADA0 + 20, 4, F_GATE0)
            norm("mix0", hT, ld["x"], 16)
            in_proj()
            norm("ffn0", hT, x_mix[0], 4 * N_SQ)
            peer_scores(0, C_PQ0)
            plain = [(1, STEPS // 2 - 2, None, 0)]
            soft(0)
            gelus(0, plain, lambda: soft(1))
            gelus(1, [(1, 14, lambda k: ada_pair(1, C_ADA1, SHIFT, k), 0)], lambda: soft(2))
            gelus(2, [(1, 2, lambda k: ada_pair(1, C_ADA1 + 28, F_GATE1, k), 0), (1, 12, None, 0)], lambda: soft(3))
            gelus(3, plain)
            act.wait_ge(x_ffn[0], NT)
            load(brow, bias_rows[0:1, 6 * D:14 * D].to_broadcast([P, 8 * D]).rearrange("p (r n) -> p r n", r=8), "bias1")
            load(gain, gains[0:1, 2 * D:5 * D].to_broadcast([P, 3 * D]).rearrange("p (r n) -> p r n", r=3), "gain1")
            load(keyT, keys[1], "keys1")
            load(fw, f_w, "fw")
            norm("kv", hT, x_ffn[0], NT)
            forget()
            project_v()
            norm("mix1", hqT, x_ffn[0], NT)
            attention()
            copies("att", hT)
            norm("ffn1", hT, x_mix[1], 4 * N_SQ)
            load(rows[:, SHIFT, :], gains[0:1, 5 * D:6 * D].to_broadcast([P, D]), "gainf")
            peer_scores(1, C_PQ1)
            soft(4)
            gelus(4, plain, lambda: soft(5))
            gelus(5, plain, lambda: soft(6))
            gelus(6, plain, lambda: soft(7))
            gelus(7, plain)
            norm("fin", None, x_ffn[1], NT)

        @block.vector
        def _(dve):
            me = Ticks(dve, dv)

            def silu():
                dve.wait_ge(silu_e, 1)
                me(dve.tensor_scalar(cs[:, 2, :], cs[:, 1, :], 1.0, None, ALU.add))
                me.sync()
                me(dve.reciprocal(cs[:, 1, :], cs[:, 2, :]))
                me.sync()
                me(dve.tensor_tensor(cs[:, 2, :], cs[:, 0, :], cs[:, 1, :], ALU.mult))
                me.sync()
                dve.tensor_copy(sB[:], cs[:, 2, :].unsqueeze(2).to_broadcast([P, KB, P])).then_inc(silu_b, 1)

            def finish_rows(plan):
                for row, b, const, _ in plan:
                    me(dve.scalar_tensor_tensor(rows[:, row, :], rows[:, row, :], const, brow[:, b, :], ALU.add, ALU.add))
                me.sync()
                for row, _, _, g in plan:
                    if g is not None:
                        me(dve.tensor_tensor(rows[:, row, :], rows[:, row, :], gain[:, g, :], ALU.mult))
                me.sync()

            def norm(name, a_row, b_row):
                dve.wait_ge(n_sq[name], NT)
                dve.tensor_scalar(stat[:, 0, :], stat[:, 0, :], 1.0 / D, EPS, ALU.mult, ALU.add).then_inc(n_ms[name], 1)
                dve.wait_ge(n_rt[name], 1)
                me(dve.reciprocal(stat[:, 0, :], stat[:, 1, :]))
                me.sync()
                if name == "fin":
                    dve.wait_ge(ld["gainf"], 16)
                    for t in range(NT):
                        dve.scalar_tensor_tensor(xs[:, t, :], xs[:, t, :], stat[:, 0, t:t + 1], rows[:, SHIFT, :],
                                                 ALU.mult, ALU.mult).then_inc(y_ok, 1)
                    return
                for t in range(NT):
                    me(dve.scalar_tensor_tensor(hs[:, t, :], xs[:, t, :], stat[:, 0, t:t + 1], rows[:, a_row, :],
                                                ALU.mult, ALU.mult))
                    if t:
                        me.sync(1)
                        dve.tensor_tensor(hs[:, t - 1, :], hs[:, t - 1, :], rows[:, b_row, :], ALU.add).then_inc(n_h[name], 1)
                me.sync()
                dve.tensor_tensor(hs[:, NT - 1, :], hs[:, NT - 1, :], rows[:, b_row, :], ALU.add).then_inc(n_h[name], 1)

            def in_proj():
                me(dve.memset(cu[:, :, 0:2], 0.0))
                me.sync()

                def body(i, first):
                    for jp in range(2):
                        J = 4 * i + 2 * jp
                        n = C_IN + 3 * jp
                        me(dve.tensor_copy(taps[:], convs[:, bass.ds(J, 2), :]))
                        w_done(dve, n + 1, 3 * i)
                        for jj in range(2):
                            dve.wait_ge(c_out, J + jj + 1)
                            dve.tensor_tensor(cu[:, jj, 2:2 + S], ps[2 + jj], c_s[:, jj, :], ALU.mult).then_inc(cu_ok, 1)
                        dve.wait_ge(cu_ok, J + 2)
                        me.sync()
                        for jj in range(2):
                            me(dve.tensor_scalar(z_s[:, jj, :], cu[:, jj, 0:S], taps[:, jj, 0:1], None, ALU.mult))
                        for w in (1, 2):
                            for jj in range(2):
                                me.sync(1)
                                me(dve.scalar_tensor_tensor(z_s[:, jj, :], cu[:, jj, w:w + S], taps[:, jj, w:w + 1],
                                                            z_s[:, jj, :], ALU.mult, ALU.add))
                        w_done(dve, n + 2, 3 * i)
                        me.sync()
                        for jj in range(2):
                            dve.tensor_tensor(gT[:, bass.ds(J + jj, 1), :].squeeze(1), ps[4 + jj], z_s[:, jj, :],
                                              ALU.mult).then_inc(g_ok, 1)
                body(0, True)
                body(1, False)

            def add_projection(L, c0, gate_row):
                def body(i, first):
                    for s in range(2):
                        w_done(dve, c0 + s, i)
                        cols = bass.ds((2 * i + s) * CW, CW)
                        done = 2 * NT * i + NT * s
                        if not first:
                            dve.wait_ge(x_mix[L], done - NT)
                        for t in range(NT):
                            dve.tensor_tensor(y_s[:, s, t, :], ps[4 * s + t][:, 0:CW], rows[:, gate_row, cols],
                                              ALU.mult).then_inc(y_in[L], 1)
                        for t in range(NT):
                            dve.wait_ge(y_in[L], done + t + 1)
                            dve.tensor_tensor(xs[:, t, cols], xs[:, t, cols], y_s[:, s, t, :], ALU.add).then_inc(x_mix[L], 1)
                peeled(dve, N_SQ // 2, body)

            LIST_STEPS, HEAD_STEPS = 23, 31
            full = [P, 4, TOPK, TOPK]

            def route_lists(T, i):
                me(dve.tensor_copy(stage, sc[:, T % NT, bass.ds(4 * i, 4), :]))
                top16([stage[:, l, :] for l in range(4)], tv4, ti4)
                me(dve.tensor_copy(tv[:, bass.ds(4 * i, 4), :], tv4))
                me(dve.tensor_copy(tif[:, bass.ds(4 * i, 4), :], ti4))
                me.sync()

            def route_heads(T, i):
                by_head = tv.rearrange("p (h c) k -> p h c k", c=2)
                idx_by_head = tif.rearrange("p (h c) k -> p h c k", c=2)
                pick1 = eq.rearrange("p (n a) -> p n a", a=TOPK)
                pick2 = hf[:, 0:1024].rearrange("p (n a) -> p n a", a=TOPK)
                hh = bass.ds(4 * i, 4)
                me(dve.tensor_tensor(cand, by_head[:, hh, 0, :].unsqueeze(3).to_broadcast(full),
                                     by_head[:, hh, 1, :].unsqueeze(2).to_broadcast(full), ALU.add))
                top16([candf[:, l, :] for l in range(4)], bv4, bp4.rearrange("p (l k) -> p l k", l=4))
                me(dve.tensor_copy(bs[:, hh, :], bv4))
                me(dve.tensor_scalar(ra4, bp4, 4, None, ALU.logical_shift_right))
                me(dve.tensor_scalar(rb4, bp4, TOPK - 1, None, ALU.bitwise_and))
                for pick, rank in ((pick1, ra4), (pick2, rb4)):
                    me.sync(0 if pick is pick1 else 1)
                    me(dve.tensor_tensor(pick, iota.unsqueeze(1).to_broadcast([P, 64, TOPK]),
                                         rank.unsqueeze(2).to_broadcast([P, 64, TOPK]), ALU.is_equal))
                for c, pick in enumerate((pick1, pick2)):
                    me.sync(1)
                    p4 = pick.rearrange("p (h k) a -> p h k a", h=4)
                    me(dve.tensor_tensor(p4, p4, idx_by_head[:, hh, c, :].unsqueeze(2).to_broadcast(full), ALU.mult))
                for pick, e in ((pick1, e1), (pick2, e2)):
                    me.sync(1)
                    me(dve.tensor_reduce(e, pick, AX_X, ALU.add))
                me.sync()
                me(dve.scalar_tensor_tensor(idx[:, T % 2, bass.ds(64 * i, 64)], e1, float(NK), e2, ALU.mult, ALU.add))
                me.sync()

            def route_gates(T):
                dve.tensor_tensor(bd, bs, bs[:, :, 0:1].to_broadcast([P, PH, TOPK]), ALU.subtract).then_inc(r_d, 1)
                dve.wait_ge(r_e, T + 1)
                me(dve.tensor_reduce(gsum[:, 0, :], bd, AX_X, ALU.add))
                me.sync()
                me(dve.reciprocal(gsum[:, 1, :], gsum[:, 0, :]))
                me.sync()
                dve.tensor_tensor(gates[:, T % 2, :].rearrange("p (h k) -> p h k", h=PH), bd,
                                  gsum[:, 1, :].unsqueeze(2).to_broadcast([P, PH, TOPK]), ALU.mult).then_inc(r_ok, 1)
                dve.wait_ge(r_ok, T + 1)

            def route(T):
                for work, times, steps in ((route_lists, LISTS // 4, LIST_STEPS), (route_heads, 2, HEAD_STEPS)):
                    with dve.Fori(0, times) as i:
                        me.enter(i, steps)
                        work(T, i)
                    me.leave(times)
                route_gates(T)

            def routing_of(T):
                return [(2, LISTS // 4, lambda k: route_lists(T, k), LIST_STEPS),
                        (2, 2, lambda k: route_heads(T, k), HEAD_STEPS), (1, 2, None, 0)]

            def top16(lists, best, where):
                def settle():
                    me.sync()
                    dve.nop(nofuse=True)
                for r in range(2):
                    w = slice(8 * r, 8 * r + 8)
                    settle()
                    for l, values in enumerate(lists):
                        me(dve.max(best[:, l, w], values))
                    settle()
                    for l, values in enumerate(lists):
                        me(dve.max_index(where[:, l, w], best[:, l, w], values))
                    if r == 0:
                        settle()
                        for l, values in enumerate(lists):
                            me(dve.match_replace(values, best[:, l, w], values, LOWEST))
                me.sync()

            def experts(T, segments, last=None):
                t, base = T % NT, T * (STEPS // 2)
                tok = hs[:, t, :]
                g = gates[:, T % 2, :]
                dve.wait_ge(r_ok, T + 1)
                for b in (6, 7):
                    me(dve.memset(ps[b], 0.0))
                me.sync()

                def dot(n, r):
                    buf = ring[:, HALF * n + r, :]
                    dve.tensor_tensor_reduce(buf, buf, tok, 1.0, 0.0, ALU.mult, ALU.add,
                                             dots[:, n, r:r + 1]).then_inc(u_used[n], 1)

                def weigh(n, f, slot):
                    dve.wait_ge(act_ok[n], f + 1)
                    dve.tensor_tensor(coef[:, n, :], acts[:, n, :], g[:, bass.ds(slot, HALF)],
                                      ALU.mult).then_inc(coef_ok[n], 1)

                def add(n, f, r, first):
                    if r:
                        dve.wait_ge(v_used[n], BY_DVE * f + r)
                    elif not first:
                        dve.wait_ge(v_used[1 - n], BY_DVE * (f + n))
                    dve.scalar_tensor_tensor(acc, ring[:, 8 + HALF * n + r, :], coef[:, n, r:r + 1], acc,
                                             ALU.mult, ALU.add).then_inc(v_used[n], 1)

                def step(nu, fu, nv, fv, slot, first=False):
                    dve.wait_ge(u_got[nu], 16 * HALF * (fu + 1))
                    dot(nu, 0)
                    weigh(nv, fv, slot)
                    dot(nu, 1)
                    dve.wait_ge(v_got[nv], 16 * HALF * (fv + 1))
                    dve.wait_ge(coef_ok[nv], fv + 1)
                    add(nv, fv, 0, first)
                    dot(nu, 2)
                    add(nv, fv, 1, first)
                    dot(nu, 3)

                dve.wait_ge(u_got[0], 16 * HALF * (base + 1))
                for r in range(HALF):
                    dot(0, r)
                step(1, base, 0, base, 0, first=True)
                step(0, base + 1, 1, base, HALF)
                def turn(i):
                    step(1, i + base, 0, i + base, 2 * HALF * i)
                    step(0, i + (base + 1), 1, i + base, 2 * HALF * i + HALF)
                window(dve, turn, segments, me)
                if last:
                    last()
                end = base + STEPS // 2 - 1
                step(1, end, 0, end, SLOTS - 2 * HALF)
                weigh(1, end, SLOTS - HALF)
                dve.wait_ge(v_got[1], 16 * HALF * (end + 1))
                dve.wait_ge(coef_ok[1], end + 1)
                for r in range(BY_DVE):
                    add(1, end, r, False)
                dve.wait_ge(v_used[1], BY_DVE * (end + 1))
                me(dve.tensor_tensor(eq, acc, rows[:, F_GATE[T // NT], :], ALU.mult))
                me.sync()
                me(dve.tensor_tensor(xs[:, t, :], xs[:, t, :], eq, ALU.add))
                me.sync()
                dve.wait_ge(v_used_pe[1], end + 1)
                me(dve.tensor_tensor(eq, acc_pe, rows[:, F_GATE[T // NT], :], ALU.mult))
                me.sync()
                dve.tensor_tensor(xs[:, t, :], xs[:, t, :], eq, ALU.add).then_inc(x_ffn[T // NT], 1)
                dve.wait_ge(x_ffn[T // NT], t + 1)

            def forget():
                me(dve.memset(aux_l, 1.0))
                dve.wait_ge(f_done, 1)
                dve.wait_ge(ld["fb"], 16)
                dve.tensor_scalar(cum, ps[0][0:FR, :], fb[:], None, ALU.add).then_inc(f_z, 1)
                dve.wait_ge(f_l, 1)
                dve.wait_ge(f_z, 1)
                me(dve.scalar_tensor_tensor(aux_b, cum, 0.0, aux_r, ALU.min, ALU.subtract))
                me.sync()
                me(dve.tensor_tensor_scan(cum, aux_l, aux_b, 0.0, ALU.mult, ALU.add))
                me.sync()
                me(dve.tensor_copy(aux_r, cum))
                me(dve.tensor_copy(aux_b, cum))
                me.sync()
                for n in (0, 64):
                    me(dve.memset(aux_b[n:n + 32, :], -1.0))
                    me(dve.memset(aux_r[n + 32:n + 48, :], 1.0))
                me.sync()

            def attention():
                def scores(i, h, first):
                    n = 4 * i + h
                    for t in range(NT):
                        dve.wait_ge(a_s, 4 * n + t + 1)
                        diag = ps[2 + t][:, t * P:(t + 1) * P]
                        me(dve.tensor_tensor(diag, diag, mask, ALU.add))
                        if t:
                            me.sync(1)
                            row_max(h, t - 1)
                    me.sync()
                    row_max(h, NT - 1)

                def row_max(h, t):
                    dve.reduce_max(amax[:, h % 2, t:t + 1], ps[2 + t][:, 0:(t + 1) * P], AX_X,
                                   negate=True).then_inc(a_max, 1)

                def aux(i, h, first):
                    n = 4 * i + h
                    rows48 = slice(64 * (h % 2), 64 * (h % 2) + 48)
                    if not (first and h < 2):
                        dve.wait_ge(a_s, 4 * (n - 1))
                    dve.tensor_tensor(aux_l[rows48, :], aux_b[rows48, :],
                                      kc[rows48, bass.ds(K_SEL + n, 1)].to_broadcast([48, S]), ALU.mult).then_inc(aux_ok, 1)

                def finish(i, h):
                    n = 4 * i + h
                    dve.wait_ge(a_exp, 4 * n + 4)
                    me(dve.reciprocal(ainv[:, h % 2, :], asum[:, h % 2, :]))
                    dve.wait_ge(a_pv, n + 1)
                    me.sync()
                    dve.tensor_tensor(hs[:, :, bass.ds(n * HD, HD)],
                                      ps[h % 2][:, 0:NT * HD].rearrange("p (t d) -> p t d", t=NT),
                                      ainv[:, h % 2, :].unsqueeze(2).to_broadcast([P, NT, HD]), ALU.mult).then_inc(a_o, 1)

                def body(i, first):
                    for h in range(4):
                        aux(i, h, first)
                        if h % 2 == 0:
                            if not (first and h == 0):
                                finish(i, h - 1) if h else finish(i - 1, 3)
                            scores(i, h, first)
                        else:
                            scores(i, h, first)
                            finish(i, h - 1)
                body(0, True)
                with dve.Fori(1, HEADS // 4) as i:
                    me.enter(i - 1, 20)
                    body(i, False)
                me.leave(HEADS // 4 - 1)
                finish(HEADS // 4 - 1, 3)

            dve.wait_ge(ld["c"], 16)
            silu()
            dve.wait_ge(ld["bias0"], 16)
            dve.wait_ge(ld["gain0"], 16)
            dve.wait_ge(ada_out[0], 12)
            finish_rows([(SHIFT, 0, 0.0, None), (SCALE, 1, 1.0, 0), (GATE, 2, 1.0, None)])
            dve.wait_ge(ld["x"], 16)
            norm("mix0", SCALE, SHIFT)
            dve.wait_ge(ada_out[0], N_ADA[0])
            finish_rows([(F_SHIFT, 3, 0.0, None), (F_SCALE, 4, 1.0, 1), (F_GATE0, 5, 1.0, None)])
            dve.wait_ge(ld["conv"], 16)
            in_proj()
            add_projection(0, C_OUT, GATE)
            norm("ffn0", F_SCALE, F_SHIFT)
            dve.wait_ge(s_out[0], LISTS)
            dve.wait_ge(ld["const"], 16)
            route(0)
            for T in range(NT - 1):
                experts(T, routing_of(T + 1), lambda: route_gates(T + 1))
            experts(NT - 1, [(1, STEPS // 2 - 2, None, 0)])
            dve.wait_ge(ld["bias1"], 16)
            dve.wait_ge(ld["gain1"], 16)
            dve.wait_ge(ada_out[1], N_ADA[1])
            finish_rows([(SHIFT, 0, 0.0, None), (SCALE, 1, 1.0, 1), (GATE, 2, 1.0, None),
                         (KV_SHIFT, 3, 0.0, None), (KV_SCALE, 4, 1.0, 0),
                         (F_SHIFT, 5, 0.0, None), (F_SCALE, 6, 1.0, 2), (F_GATE1, 7, 1.0, None)])
            norm("kv", KV_SCALE, KV_SHIFT)
            forget()
            norm("mix1", SCALE, SHIFT)
            attention()
            add_projection(1, C_WO, GATE)
            norm("ffn1", F_SCALE, F_SHIFT)
            dve.wait_ge(s_out[1], LISTS)
            route(NT)
            for T in range(NT, 2 * NT - 1):
                experts(T, routing_of(T + 1), lambda: route_gates(T + 1))
            experts(2 * NT - 1, [(1, STEPS // 2 - 2, None, 0)])
            norm("fin", None, None)

        @block.gpsimd
        def _(pool):
            def gather(kind, T, n, f, slot, first=False):
                table, at, ids, got, copied = (
                    (tables[2 * (T // NT)], 0, idx_u, u_got, ix_u) if kind == "u" else
                    (tables[2 * (T // NT) + 1], 8, idx_v, v_got, ix_v))
                if not first:
                    if kind == "u":
                        pool.wait_ge(u_used[n], HALF * f)
                    else:
                        pool.wait_ge(v_used[n], BY_DVE * f)
                        pool.nop(nofuse=True)
                        pool.wait_ge(v_used_pe[n], f)
                    pool.nop(nofuse=True)
                pool.tensor_copy(ids[:, n, :], idx[:, T % 2, bass.ds(slot, HALF)]).then_inc(copied, 1)
                pool.wait_ge(copied, 2 * f + (n + 1))
                pool.nop(nofuse=True)
                for r in range(HALF):
                    pool.indirect_dma_start(ring[:, at + HALF * n + r, :], None, table,
                                            bass.IndirectOffsetOnAxis(ap=ids[:, n, r:r + 1], axis=0)).then_inc(got[n], 16)

            def tile(T):
                base = T * (STEPS // 2)
                new = T == 0
                pool.wait_ge(r_ok, T + 1)
                gather("u", T, 0, base, 0, new)
                gather("u", T, 1, base, HALF, new)
                gather("v", T, 0, base, 0, new)
                gather("u", T, 0, base + 1, 2 * HALF)
                gather("v", T, 1, base, HALF, new)
                with pool.Fori(1, STEPS // 2 - 1) as i:
                    gather("u", T, 1, i + base, 2 * HALF * i + HALF)
                    gather("v", T, 0, i + base, 2 * HALF * i)
                    gather("u", T, 0, i + (base + 1), 2 * HALF * i + 2 * HALF)
                    gather("v", T, 1, i + base, 2 * HALF * i + HALF)
                last = base + STEPS // 2 - 1
                gather("u", T, 1, last, SLOTS - HALF)
                gather("v", T, 0, last, SLOTS - 2 * HALF)
                gather("v", T, 1, last, SLOTS - HALF)

            for T in range(2 * NT):
                tile(T)


INPUTS = ["x", "cT", "consts", "conv", "f_w", "f_bias", "bias_rows", "gains", "keys", "wstream",
          "u0", "v0", "u1", "v1"]


def kernel(**inputs):
    import numpy as np
    import concourse.bacc as bacc
    from concourse.bass_utils import run_bass_kernel_spmd as run

    a = {k: np.asarray(v) for k, v in inputs.items()}

    def chunks(w):
        return w.reshape(KB, P, -1, CW).transpose(2, 1, 0, 3).reshape(-1, P, KB * CW)

    w_in = a["a_w_in"][0].reshape(D, 3, N_SQ, CW)[:, [1, 2, 0]].transpose(0, 2, 1, 3).reshape(D, 3 * D)
    w_k, w_v, w_f = a["kv_w"][:, 0:D], a["kv_w"][:, D:2 * D], a["kv_w"][:, 2 * D:]
    w_kq = np.stack([w_k.reshape(D, KB, P), a["b_w_q"][0].reshape(D, KB, P)], axis=2).reshape(D, 2 * D)
    stream = [a["mix_ada_w"][0], a["ffn_ada_w"][0], w_in, a["a_w_out"][0], a["peer_w_q"][0],
              a["mix_ada_w"][1], a["kv_ada_w"], a["ffn_ada_w"][1], w_v, w_kq, a["b_w_o"][0], a["peer_w_q"][1]]
    consts = np.zeros((P, K_COLS), np.float32)
    consts[:, K_ID:K_ID + P] = np.eye(P)
    consts[:, K_MASK:K_MASK + P] = np.where(np.arange(P)[None, :] <= np.arange(P)[:, None], 0.0, -1.0e30)
    consts[:, K_IOTA:K_IOTA + TOPK] = np.arange(TOPK)
    for n in (0, 32, 64, 96):
        consts[n:n + HEADS, K_SEL:K_SEL + HEADS] = np.eye(HEADS)
    consts[:, K_ONE] = 1.0
    arrays = {
        "x": a["x"][0],
        "cT": a["c"].reshape(KB, P).T,
        "consts": consts,
        "conv": a["a_conv"][0].reshape(3, KB, P).transpose(2, 1, 0),
        "f_w": np.tile(w_f.reshape(KB, P, HEADS).transpose(1, 0, 2), (1, 1, FR // HEADS)),
        "f_bias": np.tile(a["f_bias"].reshape(HEADS, 1), (FR // HEADS, 1)),
        "bias_rows": np.concatenate([a["mix_ada_b"][0], a["ffn_ada_b"][0], a["mix_ada_b"][1], a["kv_ada_b"],
                                     a["ffn_ada_b"][1]]).reshape(1, -1),
        "gains": np.concatenate([a["mix_norm"][0], a["ffn_norm"][0], a["kv_norm"], a["mix_norm"][1],
                                 a["ffn_norm"][1], a["final_norm"]]).reshape(1, -1),
        "keys": a["peer_sub_keys"].reshape(2, LISTS * NK, DK).transpose(0, 2, 1),
        "wstream": np.concatenate([chunks(w) for w in stream]),
        "u0": a["peer_u"][0], "v0": a["peer_v"][0], "u1": a["peer_u"][1], "v1": a["peer_v"][1],
    }
    nc = bacc.Bacc("TRN2", target_bir_lowering=False, num_devices=1)
    arrays = {f"in_{k}": np.ascontiguousarray(arrays[k]) for k in INPUTS}
    aps = [nc.dram_tensor(k, v.shape, mybir.dt.from_np(v.dtype), kind="ExternalInput").ap() for k, v in arrays.items()]
    out = nc.dram_tensor("out_y", (S, D), F32, kind="ExternalOutput").ap()
    bass_trunk(nc, *aps[:10], aps[10:], out)
    r = run(nc, [arrays], core_ids=[0])
    return r.results[0]["out_y"].reshape(1, S, D)
```

```python
from contextlib import ExitStack

import concourse.bass as bass
from concourse import mybir

ALU = mybir.AluOpType
ACT = mybir.ActivationFunctionType
F32 = mybir.dt.float32
U32 = mybir.dt.uint32
AX_X = mybir.AxisListType.X

P = 128
D = 1024
S = 512
NT = S // P
KB = D // P
HEADS = 16
HD = D // HEADS
PH = 8
NK = 128
DK = 128
TOPK = 16
LISTS = 2 * PH
SLOTS = PH * TOPK
CW = 256
EPS = 1e-6
LOWEST = -3.0e38
FR = 112

N_FIRST = 2 * D // CW
N_ADA = (5 * D // CW, 8 * D // CW)
N_GATE = D // CW
N_IN = 3 * D // CW
N_SQ = D // CW
N_PQ = 2 * D // CW
N_KQ = 2 * D // CW
C_ADA0 = 0
C_IN = C_ADA0 + N_ADA[0] - N_FIRST
C_OUT = C_IN + N_IN
C_PQ0 = C_OUT + N_SQ
C_GATE0 = C_PQ0 + 2 * N_PQ
C_ADA1 = C_GATE0 + N_GATE
C_V = C_ADA1 + N_ADA[1]
C_KQ = C_V + 2 * N_SQ
C_WO = C_KQ + N_KQ
C_PQ1 = C_WO + N_SQ
N_CHUNKS = C_PQ1 + 2 * N_PQ
C_PQ = (C_PQ0, C_PQ1)

SHIFT, SCALE, GATE, KV_SHIFT, KV_SCALE, F_SHIFT, F_SCALE, F_GATE1, F_GATE0 = range(9)
F_GATE = (F_GATE0, F_GATE1)

K_ID, K_MASK, K_IOTA, K_SEL, K_ONE = 0, 128, 256, 272, 288
K_COLS = 289

HALF = 4
BY_PE = 2
BY_DVE = HALF - BY_PE
STEPS = SLOTS // HALF


class Ticks:

    def __init__(self, eng, sem):
        self.eng, self.sem, self.n, self.turn, self.per, self.start = eng, sem, 0, None, 0, 0

    def __call__(self, ins):
        ins.then_inc(self.sem, 1)
        self.n += 1

    def sync(self, back=0):
        n = self.n - back
        self.eng.wait_ge(self.sem, n if self.turn is None else self.turn * self.per + n)

    def enter(self, turn, per):
        self.turn, self.per, self.start = turn, per, self.n

    def leave(self, times):
        assert self.n - self.start == self.per, (self.n - self.start, self.per)
        self.n = self.start + self.per * times
        self.turn = None


def peeled(eng, times, body):
    body(0, True)
    if times > 1:
        with eng.Fori(1, times) as i:
            body(i, False)


def window(eng, turn, segments, ticks=None):
    at = 1
    for n, times, work, steps, *piece in segments:
        with eng.Fori(0, times) as k:
            if ticks:
                ticks.enter(k, steps)
            for c in range(n):
                turn(n * k + (at + c), piece and (lambda half: piece[0](k, 2 * c + half)))
            if work:
                work(k)
        if ticks:
            ticks.leave(times)
        at += n * times
    assert at == STEPS // 2 - 1


def one_by_one(*works):
    return [(1, times, work and (lambda k, work=work: work()), steps) for work, times, steps in works]


def bass_trunk(nc, x, cT, consts, conv, f_w, f_bias, bias_rows, gains, keys, wfirst, wstream, tables, out):
    with ExitStack() as ctx:
        def sb(name, shape, dt=F32):
            return ctx.enter_context(nc.sbuf_tensor(name, shape, dt))

        def sem(name):
            return ctx.enter_context(nc.semaphore(name))

        xs = sb("xs", [P, NT, D])
        hs = sb("hs", [P, NT, D])
        hT = sb("hT", [P, KB, S])
        rows = sb("rows", [P, 9, D])
        ring = sb("ring", [P, 16, D])
        wring = sb("wring", [P, 2, KB, CW])
        sc = sb("sc", [P, NT, LISTS, NK])
        kc = sb("kc", [P, K_COLS])
        cs = sb("cs", [P, 3, KB])
        sB = sb("sB", [P, KB, P])
        convs = sb("convs", [P, KB, 3])
        taps = sb("taps", [P, 2, 3])
        stat = sb("stat", [P, 2, NT])
        fb = sb("fb", [FR, 1])
        idx = sb("idx", [P, 2, SLOTS], U32)
        gates = sb("gates", [P, 2, SLOTS])
        gsum = sb("gsum", [P, 2, PH])
        bs = sb("bs", [P, PH, TOPK])[:]
        bd = sb("bd", [P, PH, TOPK])[:]
        idx_u = sb("idx_u", [P, 2, HALF], U32)
        idx_v = sb("idx_v", [P, 2, HALF], U32)
        dots = sb("dots", [P, 2, HALF])
        acts = sb("acts", [P, 2, HALF])
        coef = sb("coef", [P, 2, HALF])
        diag = sb("diag", [P, 2, BY_PE, P])
        amax = sb("amax", [P, 2, NT])
        asum = sb("asum", [P, 2, NT])
        ainv = sb("ainv", [P, 2, NT])
        psum = ctx.enter_context(nc.psum_tensor("psum", [P, 8, 512], F32))
        ps = [psum[:, b, :] for b in range(8)]
        acc = psum[:, 6:8, :].rearrange("p a b -> p (a b)")
        acc_pe = psum[:, 4:6, :].rearrange("p a b -> p (a b)")

        ident = kc[:, K_ID:K_ID + P]
        mask = kc[:, K_MASK:K_MASK + P]
        iota = kc[:, K_IOTA:K_IOTA + TOPK]
        one = kc[:, K_ONE:K_ONE + 1]

        brow0, gain0 = ring[:, 0:5, :], ring[:, 8:10, :]
        fw = ring[:, 13, 0:KB * FR].rearrange("p (k n) -> p k n", k=KB)
        keyT = rows[:, 3:5, :].rearrange("p a b -> p (a b)")
        c_s = ring[:, 10, :].rearrange("p (j t) -> p j t", j=2)
        cu = ring[:, 11:13, :].rearrange("p a b -> p (a b)")[:, 0:2 * (S + 2)].rearrange("p (j t) -> p j t", j=2)
        z_s = ring[:, 13, :].rearrange("p (j t) -> p j t", j=2)
        y_s = ring[:, 12:14, :].rearrange("p s (t n) -> p s t n", t=NT)
        qs_first = sc[:, NT - 1, 0:2, :]
        qs_rest = sc[:, 0, 0:8, :].rearrange("p l k -> p (l k)")[:, 0:2 * (S - P)].rearrange("p (j t) -> p j t", j=2)
        gT = hs[:].rearrange("p t n -> p (t n)").rearrange("p (k t) -> p k t", k=KB)
        hqT = ring[:, 0:4, :].rearrange("p a b -> p (a b)").rearrange("p (k t) -> p k t", k=KB)
        scf = sc[:].rearrange("p a b c -> p (a b c)")
        first_chunks = ([scf[:, n * KB * CW:(n + 1) * KB * CW] for n in range(4)] +
                        [hT[:].rearrange("p a b -> p (a b)")[:, n * KB * CW:(n + 1) * KB * CW] for n in range(2)] +
                        [ring[:, n:n + 2, :].rearrange("p a b -> p (a b)") for n in (10, 12)])
        brow1 = scf.rearrange("p (r n) -> p r n", n=D)
        gain1 = hT[:].rearrange("p a b -> p (a b)")[:, 0:3 * D].rearrange("p (r n) -> p r n", n=D)
        FEW = NT - 1
        hq_early = scf[:, 2048:2048 + FEW * D].rearrange("p (k t) -> p k t", k=KB)
        v_early = scf[:, 5120:5120 + FEW * D].rearrange("p (t n) -> p t n", n=D)
        v_late = ring[:, 10, :]
        kq_head = [ring[:, 11:13, :].rearrange("p a (b t) -> p a b t", b=2),
                   ring[:, 14:16, :].rearrange("p a (b t) -> p a b t", b=2)]
        OWN = (slice(0, HD), slice(HD, P))
        TERMS = (slice(64, 112), slice(0, 48))
        USED = (slice(0, 112), slice(0, P))

        cum = scf[0:FR, 0:512]
        aux_r = scf[0:FR, 512:1024]
        aux_b = scf[0:FR, 1024:1536]
        aux_l = scf[0:FR, 1536:2048]
        T_OFF = [0, 128, 384, 768]
        UNITS = [(0, 1), (2,), (3,)]
        U_COL = [0, P, 0, 0]
        UPTO = [u[-1] + 1 for u in UNITS]
        NU = len(UNITS)
        prob = ring[:, 4:7, :].rearrange("p a b -> p (a b)")[:, 0:2560].rearrange("p (a b) -> p a b", a=2)
        probT = ring[:, 7:9, :].rearrange("p a b -> p (a b)")[:, 0:1280]

        class Scratch:
            def __init__(self, mem):
                def cut(a, b, **dims):
                    return mem[:, a:b].rearrange("p (l k) -> p l k", **dims) if dims else mem[:, a:b]
                self.cand = mem[:, 0:1024].rearrange("p (h a b) -> p h a b", h=4, a=TOPK)
                self.candf = cut(0, 1024, l=4)
                self.pick1, self.pick2 = cut(1024, 2048, k=TOPK), cut(0, 1024, k=TOPK)
                self.eq = cut(1024, 2048)
                self.stage = cut(1024, 1536, l=4)
                self.tv, self.tif = cut(2048, 2304, l=LISTS), cut(2304, 2560, l=LISTS)
                self.tv4, self.ti4 = cut(2560, 2624, l=4), cut(2624, 2688, l=4).bitcast(U32)
                self.bv4, self.bp4 = cut(2688, 2752, l=4), cut(2752, 2816).bitcast(U32)
                self.ra4, self.rb4 = cut(2816, 2880).bitcast(U32), cut(2880, 2944).bitcast(U32)
                self.e1, self.e2 = cut(2944, 3008), cut(3008, 3072)

        in_rows = Scratch(rows[:, 0:3, :].rearrange("p a b -> p (a b)"))
        in_hT = Scratch(hT[:].rearrange("p a b -> p (a b)"))

        def scratch_for(T):
            return in_rows if T % NT < 2 else in_hT

        names = ("x c const conv fw fb biasg bias0 gain0 keys0 bias1 gain1 keys1 gainf").split()
        ld = {n: sem("ld_" + n) for n in names}
        w_got = [sem(f"w_got{s}") for s in range(2)]
        w_used = [sem(f"w_used{s}") for s in range(2)]
        dv, av = sem("dv"), sem("av")
        silu_e, silu_b = sem("silu_e"), sem("silu_b")
        ld_first = [sem(f"ld_first{n}") for n in range(N_FIRST)]
        ada_mm = sem("ada_mm")
        gate_out = sem("gate_out")
        ada_out = [sem(f"ada_out{i}") for i in range(2)]
        x_mix = [sem(f"x_mix{i}") for i in range(2)]
        x_ffn = [sem(f"x_ffn{i}") for i in range(2)]
        NORMS = ["mix0", "ffn0", "kv", "mix1", "ffn1", "fin"]
        ROOTS = ["mix0", "ffn0", "kv", "ffn1", "fin"]
        n_sq = {n: sem(f"sumsq_{n}") for n in ROOTS}
        n_ms = {n: sem(f"meansq_{n}") for n in ROOTS}
        n_rt = {n: sem(f"root_{n}") for n in ROOTS}
        n_h = {n: sem(f"h_{n}") for n in NORMS}
        n_tr = {n: sem(f"tr_{n}") for n in NORMS + ["att"]}
        n_hT = {n: sem(f"hT_{n}") for n in NORMS + ["att"]}
        c_out, cu_ok, g_ok = sem("c_out"), sem("cu_ok"), sem("g_ok")
        y_in = [sem(f"y_in{i}") for i in range(2)]
        q_mm = [sem(f"q_mm{i}") for i in range(2)]
        q_out = [sem(f"q_out{i}") for i in range(2)]
        s_done = [sem(f"s_done{i}") for i in range(2)]
        s_out = [sem(f"s_out{i}") for i in range(2)]
        f_done, f_z, f_l = sem("f_done"), sem("f_z"), sem("f_l")
        v_out = sem("v_out")
        hq_ok = sem("hq_ok")
        k_mm = sem("k_mm")
        k_out = sem("k_out")
        aux_ok, a_s, a_max, a_exp = sem("aux_ok"), sem("a_s"), sem("a_max"), sem("a_exp")
        a_tr, a_trc, a_pv, a_o = sem("a_tr"), sem("a_trc"), sem("a_pv"), sem("a_o")
        r_d, r_e, r_ok = sem("r_d"), sem("r_e"), sem("r_ok")
        u_got = [sem(f"u_got{n}") for n in range(2)]
        v_got = [sem(f"v_got{n}") for n in range(2)]
        u_used = [sem(f"u_used{n}") for n in range(2)]
        v_used = [sem(f"v_used{n}") for n in range(2)]
        v_used_pe = [sem(f"v_used_pe{n}") for n in range(2)]
        coef_ok = [sem(f"coef_ok{n}") for n in range(2)]
        diag_ok = [sem(f"diag_ok{n}") for n in range(2)]
        ix_u, ix_v = sem("ix_u"), sem("ix_v")
        act_ok = [sem(f"act_ok{n}") for n in range(2)]
        y_ok, stored = sem("y_ok"), sem("stored")

        block = ctx.enter_context(nc.Block())

        def w_ready(eng, n, i=0):
            eng.wait_ge(w_got[n % 2], 16 * (n // 2 + 1) + 16 * i)

        def w_done(eng, n, i=0):
            eng.wait_ge(w_used[n % 2], n // 2 + 1 + i)

        @block.sync
        def _(sp):
            for n in range(N_FIRST):
                sp.dma_start(first_chunks[n], wfirst[n]).then_inc(ld_first[n], 16)
            def chunks(i, first):
                for s in range(2):
                    if not first:
                        sp.wait_ge(w_used[s], i)
                    sp.dma_start(wring[:, s].rearrange("p k n -> p (k n)"),
                                 wstream[2 * i + s]).then_inc(w_got[s], 16)
            peeled(sp, N_CHUNKS // 2, chunks)
            out_tiles = out.rearrange("(t p) d -> p t d", p=P)
            sp.wait_ge(y_ok, FEW)
            sp.dma_start(out_tiles[:, 0:FEW, :], xs[:, 0:FEW, :]).then_inc(stored, 16)
            sp.wait_ge(y_ok, NT)
            sp.dma_start(out_tiles[:, FEW:NT, :], xs[:, FEW:NT, :]).then_inc(stored, 16)
            sp.wait_ge(stored, 32)

        @block.tensor
        def _(pe):
            def row_product(bank, w):
                for k in range(KB):
                    mm = pe.matmul(ps[bank][:, 0:CW], sB[:, k, :], w[:, k, :], start=(k == 0), stop=(k == KB - 1))
                return mm

            def ada_first():
                for n in range(N_FIRST):
                    pe.wait_ge(ld_first[n], 16)
                    if n >= 2:
                        pe.wait_ge(ada_out[0], n - 1)
                    row_product(n % 2, first_chunks[n].rearrange("p (k n) -> p k n", k=KB)).then_inc(ada_mm, 1)

            def ada_pair(which, pair, i=0):
                before = (N_FIRST, 0)[which]
                for s in range(2):
                    w_ready(pe, (C_ADA0, C_ADA1)[which] + 2 * pair + s, i)
                    if pair or before:
                        pe.wait_ge(ada_out[which], 2 * i + (2 * pair - 1 + s + before))
                    row_product(s, wring[:, s]).then_inc(w_used[s], 1)

            def gate_pair(pair):
                for s in range(2):
                    w_ready(pe, C_GATE0 + 2 * pair + s)
                    if pair == 0 and s == 0:
                        pe.wait_ge(q_out[0], 2 * LISTS)
                        pe.wait_ge(s_out[0], 2 * LISTS)
                    row_product(2 * pair + s, wring[:, s]).then_inc(w_used[s], 1)

            def transposes(name, src, ready, tiles=range(NT)):
                for t in tiles:
                    ready(t)
                    for half in range(2):
                        b = 4 + 2 * (t % 2) + half
                        if t >= 2:
                            pe.wait_ge(n_hT[name], 2 * (t - 2) + half + 1)
                        for j in range(4):
                            k = 4 * half + j
                            mm = pe.transpose(ps[b][:, j * P:(j + 1) * P], src[:, t, k * P:(k + 1) * P], ident)
                        mm.then_inc(n_tr[name], 1)

            def norm_T(name, tiles=range(NT)):
                transposes(name, hs, lambda t: pe.wait_ge(n_h[name], t + 1), tiles)

            def in_proj():
                pe.wait_ge(n_hT["mix0"], 2 * NT)
                pe.wait_ge(ada_out[0], N_ADA[0])

                def body(i, first):
                    for jp in range(2):
                        for third in range(3):
                            n = C_IN + 3 * jp + third
                            w_ready(pe, n, 3 * i)
                            if not (first and jp == 0):
                                s_free = (c_out, cu_ok, g_ok)[third]
                                pe.wait_ge(s_free, 4 * i + 2 * jp)
                            for jj in range(2):
                                for k in range(KB):
                                    mm = pe.matmul(ps[2 * third + jj], wring[:, n % 2, k, jj * P:(jj + 1) * P],
                                                   hT[:, k, :], start=(k == 0), stop=(k == KB - 1))
                            mm.then_inc(w_used[n % 2], 1)
                peeled(pe, 2, body)

            def project(src, c0, free):
                def body(i, first):
                    for s in range(2):
                        w_ready(pe, c0 + s, i)
                        for t in range(NT):
                            if not first:
                                pe.wait_ge(free, 4 * (2 * i + s - 2) + t + 1)
                            for k in range(KB):
                                mm = pe.matmul(ps[4 * s + t][:, 0:CW], src[:, k, t * P:(t + 1) * P],
                                               wring[:, s, k, :], start=(k == 0), stop=(k == KB - 1))
                        mm.then_inc(w_used[s], 1)
                peeled(pe, N_SQ // 2, body)

            def score_piece(L, rest, i, c, old=True, new=True, fresh=False):
                j, n = (4 * i + c) + LISTS * rest, S - P if rest else P
                qs = qs_rest if rest else qs_first
                if new:
                    if not (fresh and c < 2):
                        pe.wait_ge(q_out[L], j - 1)
                    w_ready(pe, C_PQ[L] + N_PQ * rest + c // 2, i)
                    for k in range(KB):
                        mm = pe.matmul(ps[c % 2][:, 0:n], wring[:, c // 2, k, c % 2 * P:(c % 2 + 1) * P],
                                       hT[:, k, rest * P:rest * P + n], start=(k == 0), stop=(k == KB - 1))
                    mm.then_inc(w_used[c // 2] if c % 2 else q_mm[L], 1)
                if old:
                    pe.wait_ge(q_out[L], j - 1)
                    if not (fresh and c < 4):
                        pe.wait_ge(s_out[L], j - 3)
                    for t in range(n // P):
                        mm = pe.matmul(ps[2 + c % 2][:, t * P:(t + 1) * P], qs[:, c % 2, t * P:(t + 1) * P],
                                       keyT[:, bass.ds((4 * i + c - 2) * NK, NK)], start=True, stop=True)
                    mm.then_inc(s_done[L], 1)

            def first_scores(L):
                pe.wait_ge(n_hT[f"ffn{L}"], 2)
                pe.wait_ge(ld[f"keys{L}"], 16)
                for c in range(4):
                    score_piece(L, 0, 0, c, old=c >= 2, fresh=True)
                with pe.Fori(1, LISTS // 4) as i:
                    for c in range(4):
                        score_piece(L, 0, i, c)
                for c in range(2):
                    score_piece(L, 0, LISTS // 4, c, new=False)

            def rest_scores(L):
                return [(2, 1, None, 0, lambda k, c: score_piece(L, 1, k, c, old=c >= 2)),
                        (2, 3, None, 0, lambda k, c: score_piece(L, 1, k + 1, c)),
                        (1, 1, None, 0, lambda k, c: score_piece(L, 1, LISTS // 4, c, new=False))]

            def mix_T(name, tile, t, banks):
                pe.wait_ge(n_h[name], t + 1)
                for half in range(2):
                    for j in range(4):
                        k = 4 * half + j
                        mm = pe.transpose(ps[banks[half]][:, j * P:(j + 1) * P], hs[:, tile, k * P:(k + 1) * P], ident)
                    mm.then_inc(n_tr[name], 1)

            def early_work():
                def kv_01():
                    pe.wait_ge(ada_out[1], N_ADA[1])
                    mix_T("kv", 0, 0, (0, 1))
                    mix_T("kv", 1, 1, (2, 3))

                def kv_2():
                    pe.wait_ge(n_hT["kv"], 2)
                    mix_T("kv", 2, 2, (0, 1))

                def v_chunk(n):
                    if n == 0:
                        pe.wait_ge(n_hT["kv"], 2 * FEW)
                    w_ready(pe, C_V + n)
                    for t in range(FEW):
                        if n:
                            pe.wait_ge(v_out, FEW * (n - 1) + t + 1)
                        for k in range(KB):
                            mm = pe.matmul(ps[t][:, 0:CW], hT[:, k, t * P:(t + 1) * P], wring[:, n % 2, k, :],
                                           start=(k == 0), stop=(k == KB - 1))
                    mm.then_inc(w_used[n % 2], 1)

                def mix_01():
                    pe.wait_ge(v_out, FEW * N_SQ)
                    mix_T("mix1", 0, 0, (0, 1))
                    mix_T("mix1", 1, 1, (2, 3))

                def mix_2():
                    pe.wait_ge(n_hT["mix1"], 2)
                    mix_T("mix1", 2, 2, (0, 1))
                return one_by_one((None, 4, 0), (kv_01, 1, 0), (None, 1, 0), (kv_2, 1, 0),
                                  *[(lambda n=n: v_chunk(n), 1, 0) for n in range(N_SQ)],
                                  (mix_01, 1, 0), (mix_2, 1, 0), (None, 1, 0))

            def late_work():
                pe.wait_ge(n_hT["kv"], 2 * FEW)
                pe.wait_ge(n_hT["mix1"], 2 * FEW)
                mix_T("kv", 3, 3, (0, 1))
                mix_T("mix1", 0, 3, (2, 3))
                forget()
                pe.wait_ge(x_ffn[0], NT)
                for n in range(N_SQ):
                    w_ready(pe, C_V + N_SQ + n)
                    for k in range(KB):
                        mm = pe.matmul(ps[4 + n][:, 0:CW], hT[:, k, FEW * P:S], wring[:, n % 2, k, :],
                                       start=(k == 0), stop=(k == KB - 1))
                    mm.then_inc(w_used[n % 2], 1)
                pe.wait_ge(f_z, 1)

            def forget():
                pe.wait_ge(n_hT["kv"], 2 * NT)
                pe.wait_ge(ld["fw"], 16)
                for k in range(KB):
                    mm = pe.matmul(ps[0][0:FR, :], fw[:, k, :], hT[:, k, :], start=(k == 0), stop=(k == KB - 1))
                mm.then_inc(f_done, 1)

            def attention():
                pe.wait_ge(n_hT["mix1"], 2 * NT)
                pe.wait_ge(hq_ok, 1)
                pe.wait_ge(v_out, 4 * N_SQ)
                parts = [range(0, 3), range(3, 6), range(6, KB)]

                def kq_part(i, c, q, ks, new=False):
                    s, j = c % 2, 2 * i + c
                    if ks[0] == 0:
                        if not (new and not q):
                            pe.wait_ge(k_out, 2 * j + q)
                        if not q:
                            w_ready(pe, C_KQ + s, i + c // 2)
                    for k in ks:
                        mm = pe.matmul(ps[0], wring[:, s, k, q * P:(q + 1) * P], (hT, hqT)[q][:, k, :],
                                       start=(k == 0), stop=(k == KB - 1))
                    if ks[-1] == KB - 1:
                        mm.then_inc(w_used[s] if q else k_mm, 1)

                def scores(i, c, u, new):
                    n, s, kq, used = 4 * i + c, c // 2, kq_head[c % 2], USED[c % 2]
                    if u == 0:
                        if c % 2 == 0:
                            pe.wait_ge(k_out, n + 2)
                        pe.wait_ge(aux_ok, n + 1)
                    if not new:
                        pe.wait_ge(a_exp, 4 * n - 4 + UPTO[u])
                    for t in UNITS[u]:
                        ke, o = (t + 1) * P, U_COL[t]
                        mm = pe.matmul(ps[2 + u][:, o:o + ke], kq[used, s, 1, t * P:ke], kq[used, s, 0, 0:ke],
                                       start=True, stop=True)
                    mm.then_inc(a_s, 1)

                def turn_probs(i, c, u, new):
                    n, m = 4 * i + c, NU * c + u
                    pe.wait_ge(a_exp, 4 * n + UPTO[u])
                    if not (new and m < 2):
                        pe.wait_ge(a_trc, NU * 4 * i + m - 1)
                    base = T_OFF[UNITS[u][0]]
                    for t in UNITS[u]:
                        for kb in range(t + 1):
                            o = T_OFF[t] + kb * P
                            mm = pe.transpose(ps[6 + m % 2][:, o - base:o - base + P], prob[:, c % 2, o:o + P], ident)
                    mm.then_inc(a_tr, 1)

                def values(i, c, u, new):
                    n, m = 4 * i + c, NU * c + u
                    pe.wait_ge(a_trc, NU * 4 * i + m + 1)
                    if u == 0 and not (new and c < 2):
                        pe.wait_ge(a_o, n - 1)
                    for t in UNITS[u]:
                        for kb in range(t + 1):
                            o = T_OFF[t] + kb * P
                            mm = pe.matmul(ps[(1, 5)[c % 2]][:, t * HD:(t + 1) * HD], probT[:, o:o + P],
                                           (v_early[:, kb, :] if kb < FEW else v_late)[:, bass.ds(n * HD, HD)], start=(kb == 0), stop=(kb == t))
                    mm.then_inc(a_pv, 1)

                def step(i, c, u, new=False, last=False, only_values=False):
                    if not (new and c == 0):
                        turn_probs(i, c - 1, u, new and c == 1)
                    if u:
                        if not (new and c == 0):
                            values(i, c - 1, u - 1, new)
                    elif not (new and c < 2):
                        values(i, c - 2, NU - 1, new)
                    if not only_values:
                        scores(i, c, u, new and c == 0)
                        if not (last and c >= 2):
                            kq_part(i, c // 2 + 1, c % 2, parts[u])

                def body(i, new=False, last=False):
                    for c in range(4):
                        for u in range(NU):
                            step(i, c, u, new, last)
                kq_part(0, 0, 0, range(KB), True)
                kq_part(0, 0, 1, range(KB), True)
                body(0, new=True)
                with pe.Fori(1, HEADS // 4 - 1) as i:
                    body(i)
                body(HEADS // 4 - 1, last=True)
                for u in range(NU):
                    step(HEADS // 4, 0, u, only_values=True)
                values(HEADS // 4, -1, NU - 1, False)

            def add_rows(T, segments):
                base = T * (STEPS // 2)

                def half(n, f, start=False, stop=False):
                    pe.wait_ge(v_got[n], 16 * HALF * (f + 1))
                    pe.wait_ge(diag_ok[n], BY_PE * (f + 1))
                    for j in range(BY_PE):
                        for c in range(2):
                            mm = pe.matmul(ps[4 + c], diag[:, n, j, :],
                                           ring[:, 8 + HALF * n + BY_DVE + j, c * 512:(c + 1) * 512],
                                           start=start and j == 0, stop=stop and j == BY_PE - 1,
                                           skip_group_check=True)
                    mm.then_inc(v_used_pe[n], 1)

                def turn(i, piece):
                    half(0, i + base)
                    if piece:
                        piece(0)
                    half(1, i + base)
                    if piece:
                        piece(1)
                if T % NT:
                    pe.wait_ge(x_ffn[T // NT], T % NT)
                half(0, base, start=True)
                half(1, base)
                window(pe, turn, segments)
                end = base + STEPS // 2 - 1
                half(0, end)
                half(1, end, stop=True)

            pe.wait_ge(silu_b, 1)
            ada_first()
            with pe.Fori(0, (N_ADA[0] - N_FIRST) // 2) as i:
                ada_pair(0, 0, i)
            pe.wait_ge(ld["const"], 16)
            norm_T("mix0")
            in_proj()
            pe.wait_ge(g_ok, KB)
            project(gT, C_OUT, y_in[0])
            pe.wait_ge(y_in[0], 4 * N_SQ)
            norm_T("ffn0", [0])
            first_scores(0)
            norm_T("ffn0", [1, 2, 3])
            pe.wait_ge(n_hT["ffn0"], 2 * NT)
            plain = [(1, STEPS // 2 - 2, None, 0)]
            add_rows(0, rest_scores(0) + one_by_one((None, 2, 0), (lambda: gate_pair(0), 1, 0),
                                                    (lambda: gate_pair(1), 1, 0), (None, 1, 0)))
            pe.wait_ge(gate_out, N_GATE)
            ada_pair(1, 0)
            add_rows(1, [(1, 14, lambda k: ada_pair(1, 1, k), 0)])
            add_rows(2, [(1, 1, lambda k: ada_pair(1, 15, k), 0), (1, 13, None, 0)])
            add_rows(3, early_work())
            late_work()
            attention()
            pe.wait_ge(a_o, HEADS)
            transposes("att", hs, lambda t: None)
            pe.wait_ge(n_hT["att"], 2 * NT)
            project(hT, C_WO, y_in[1])
            pe.wait_ge(y_in[1], 4 * N_SQ)
            norm_T("ffn1", [0])
            first_scores(1)
            norm_T("ffn1", [1, 2, 3])
            pe.wait_ge(n_hT["ffn1"], 2 * NT)
            add_rows(NT, rest_scores(1) + one_by_one((None, 5, 0)))
            for T in range(NT + 1, 2 * NT):
                add_rows(T, plain)

        @block.scalar
        def _(act):
            def load(dst, src, name):
                act.dma_start(dst, src).then_inc(ld[name], 16)

            me = Ticks(act, av)

            flat_rows = rows[:].rearrange("p r n -> p (r n)")

            def ada_pair(which, c0, row0, i):
                for s in range(2):
                    w_done(act, c0 + s, i)
                    act.activation(flat_rows[:, bass.ds(row0 * D + (2 * i + s) * CW, CW)], ps[s][:, 0:CW],
                                   ACT.Copy).then_inc(ada_out[which], 1)

            def ada_first():
                for n in range(N_FIRST):
                    act.wait_ge(ada_mm, n + 1)
                    act.activation(flat_rows[:, n * CW:(n + 1) * CW], ps[n % 2][:, 0:CW],
                                   ACT.Copy).then_inc(ada_out[0], 1)

            def ada0(c0, n, row0):
                with act.Fori(0, n // 2) as i:
                    ada_pair(0, c0, row0, i)

            def copies(name, dst, tiles=range(NT)):
                for t in tiles:
                    for half in range(2):
                        b = 4 + 2 * (t % 2) + half
                        act.wait_ge(n_tr[name], 2 * t + half + 1)
                        act.activation(dst[:, 4 * half:4 * half + 4, t * P:(t + 1) * P],
                                       ps[b].rearrange("p (j t) -> p j t", j=4), ACT.Copy).then_inc(n_hT[name], 1)

            def norm(name, dst, x_sem, x_count, tiles=range(NT)):
                act.wait_ge(x_sem, x_count)
                for t in range(NT):
                    act.activation(hs[:, t, :], xs[:, t, :], ACT.Square,
                                   accum_out=stat[:, 0, t:t + 1]).then_inc(n_sq[name], 1)
                act.wait_ge(n_ms[name], 1)
                act.activation(stat[:, 1, :], stat[:, 0, :], ACT.Sqrt).then_inc(n_rt[name], 1)
                copies(name, dst, tiles)

            def in_proj():
                def body(i, first):
                    for jp in range(2):
                        n = C_IN + 3 * jp
                        w_done(act, n, 3 * i)
                        if not (first and jp == 0):
                            act.wait_ge(cu_ok, 4 * i + 2 * jp)
                        for jj in range(2):
                            act.activation(c_s[:, jj, :], ps[jj], ACT.Copy).then_inc(c_out, 1)
                peeled(act, 2, body)

            def score_piece(L, rest, i, c, q=True, s=True, fresh=False):
                j, n = (4 * i + c) + LISTS * rest, S - P if rest else P
                qs = qs_rest if rest else qs_first
                if q:
                    b = (c - 1) % 2
                    if b:
                        w_done(act, C_PQ[L] + N_PQ * rest + (c - 2) // 2, i)
                    else:
                        act.wait_ge(q_mm[L], 2 * i + (c // 2 + 1 if c else 0) + LISTS // 2 * rest)
                    if not fresh or c >= 3:
                        act.wait_ge(s_done[L], j - 2)
                    act.activation(qs[:, b, 0:n], ps[b][:, 0:n], ACT.Copy).then_inc(q_out[L], 1)
                if s:
                    act.wait_ge(s_done[L], j - 2)
                    act.activation(sc[:, rest:rest + n // P, 4 * i + c - 3, :],
                                   ps[2 + (c - 3) % 2][:, 0:n].rearrange("p (t k) -> p t k", k=P),
                                   ACT.Copy).then_inc(s_out[L], 1)

            def first_scores(L):
                for c in range(4):
                    score_piece(L, 0, 0, c, q=c >= 1, s=c >= 3, fresh=True)
                with act.Fori(1, LISTS // 4) as i:
                    for c in range(4):
                        score_piece(L, 0, i, c)
                for c in range(3):
                    score_piece(L, 0, LISTS // 4, c, q=c < 1)

            def rest_scores(L):
                return [(2, 1, None, 0, lambda k, c: score_piece(L, 1, k, c, q=c >= 1, s=c >= 3)),
                        (2, 3, None, 0, lambda k, c: score_piece(L, 1, k + 1, c)),
                        (2, 1, None, 0, lambda k, c: score_piece(L, 1, LISTS // 4, c, q=c < 1, s=c < 3)),
                        (1, 4, None, 0)]

            def soft(T):
                act.wait_ge(r_d, T + 1)
                act.activation(bd, bd, ACT.Exp).then_inc(r_e, 1)

            def gelus(T, segments, last=None):
                base = T * (STEPS // 2)

                def half(n, f):
                    act.wait_ge(u_used[n], HALF * (f + 1))
                    act.activation(acts[:, n, :], dots[:, n, :], ACT.Gelu_apprx_tanh).then_inc(act_ok[n], 1)

                def spread(n, f, new=False):
                    act.wait_ge(coef_ok[n], f + 1)
                    if not new:
                        act.wait_ge(v_used_pe[n], f)
                    for j in range(BY_PE):
                        act.activation(diag[:, n, j, :], ident, ACT.Copy,
                                       scale=coef[:, n, BY_DVE + j:BY_DVE + j + 1]).then_inc(diag_ok[n], 1)

                def turn(i, piece, new=False):
                    spread(0, i + base, new)
                    half(1, i + base)
                    if piece:
                        piece(0)
                    spread(1, i + base, new)
                    half(0, i + (base + 1))
                    if piece:
                        piece(1)
                half(0, base)
                turn(0, None, T == 0)
                window(act, turn, segments)
                if last:
                    last()
                end = base + STEPS // 2 - 1
                spread(0, end)
                half(1, end)
                spread(1, end)

            def forget():
                act.wait_ge(f_z, 1)
                me(act.activation(aux_r, cum, ACT.Abs))
                me.sync()
                me(act.activation(aux_b, aux_r, ACT.Exp, scale=-1.0))
                me.sync()
                act.activation(aux_r, aux_b, ACT.Ln, bias=one[0:FR, :]).then_inc(f_l, 1)

            def mix_copies(name, dst, t, banks):
                for half in range(2):
                    act.wait_ge(n_tr[name], 2 * t + half + 1)
                    act.activation(dst[:, 4 * half:4 * half + 4, t * P:(t + 1) * P],
                                   ps[banks[half]].rearrange("p (j t) -> p j t", j=4), ACT.Copy).then_inc(n_hT[name], 1)

            def squares(name, tiles):
                for t in tiles:
                    act.activation(hs[:, t, :], xs[:, t, :], ACT.Square,
                                   accum_out=stat[:, 0, t:t + 1]).then_inc(n_sq[name], 1)

            def roots(name, tiles, n):
                act.wait_ge(n_ms[name], n)
                act.activation(stat[:, 1, tiles], stat[:, 0, tiles], ACT.Sqrt).then_inc(n_rt[name], 1)

            def early_work():
                def kv_01():
                    mix_copies("kv", hT, 0, (0, 1))
                    mix_copies("kv", hT, 1, (2, 3))

                def v_chunk(n):
                    w_done(act, C_V + n)
                    for t in range(FEW):
                        act.activation(v_early[:, t, n * CW:(n + 1) * CW], ps[t][:, 0:CW], ACT.Copy).then_inc(v_out, 1)

                def mix_01():
                    mix_copies("mix1", hq_early, 0, (0, 1))
                    mix_copies("mix1", hq_early, 1, (2, 3))
                return one_by_one((lambda: squares("kv", range(FEW)), 1, 0), (None, 1, 0),
                                  (lambda: roots("kv", slice(0, FEW), 1), 1, 0), (None, 2, 0),
                                  (kv_01, 1, 0), (None, 1, 0), (lambda: mix_copies("kv", hT, 2, (0, 1)), 1, 0),
                                  *[(lambda n=n: v_chunk(n), 1, 0) for n in range(N_SQ)],
                                  (mix_01, 1, 0), (lambda: mix_copies("mix1", hq_early, 2, (0, 1)), 1, 0))

            def late_work():
                squares("kv", [FEW])
                roots("kv", slice(FEW, NT), 2)
                mix_copies("kv", hT, 3, (0, 1))
                mix_copies("mix1", hqT, 3, (2, 3))
                forget()
                for n in range(N_SQ):
                    w_done(act, C_V + N_SQ + n)
                    act.activation(v_late[:, n * CW:(n + 1) * CW], ps[4 + n][:, 0:CW], ACT.Copy).then_inc(v_out, 1)

            def attention():
                def k_copy(i, c, new=False):
                    j = 2 * i + c
                    act.wait_ge(k_mm, j + 1)
                    if not new:
                        act.wait_ge(a_s, 2 * NU * j - 2 * NU)
                    act.activation(kq_head[0][OWN[0], c % 2, 0, :], ps[0][OWN[0], :], ACT.Copy)
                    act.activation(kq_head[1][OWN[1], c % 2, 0, :], ps[0][OWN[1], :], ACT.Copy).then_inc(k_out, 1)

                def q_copy(i, c):
                    w_done(act, C_KQ + c % 2, i + c // 2)
                    act.activation(kq_head[0][OWN[0], c % 2, 1, :], ps[0][OWN[0], :], ACT.Copy, scale=HD ** -0.5)
                    act.activation(kq_head[1][OWN[1], c % 2, 1, :], ps[0][OWN[1], :], ACT.Copy,
                                   scale=HD ** -0.5).then_inc(k_out, 1)

                def exps(i, c, u, new):
                    n = 4 * i + c
                    if not (new and c < 2):
                        act.wait_ge(a_tr, NU * n + (u + 1 - 2 * NU))
                    act.wait_ge(a_max, 4 * n + UPTO[u])
                    for t in UNITS[u]:
                        ke, o = (t + 1) * P, U_COL[t]
                        act.activation(prob[:, c % 2, T_OFF[t]:T_OFF[t] + ke], ps[2 + u][:, o:o + ke], ACT.Exp,
                                       bias=amax[:, c % 2, t:t + 1],
                                       accum_out=asum[:, c % 2, t:t + 1]).then_inc(a_exp, 1)

                def probs_T(i, c, u, new):
                    m = NU * c + u
                    if not new:
                        act.wait_ge(a_pv, NU * 4 * i + (m - NU + 1))
                    act.wait_ge(a_tr, NU * 4 * i + m + 1)
                    lo, hi = T_OFF[UNITS[u][0]], T_OFF[UNITS[u][-1]] + UPTO[u] * P
                    act.activation(probT[:, lo:hi], ps[6 + m % 2][:, 0:hi - lo], ACT.Copy).then_inc(a_trc, 1)

                def body(i, new=False, last=False):
                    for c in range(4):
                        for u in range(NU):
                            if u == 0:
                                if c % 2:
                                    if not (last and c == 3):
                                        k_copy(i, c // 2 + 1, new and c == 1)
                                elif not (new and c == 0):
                                    q_copy(i, c // 2)
                            exps(i, c, u, new)
                            if not (new and c == 0):
                                probs_T(i, c - 1, u, new and c == 1)
                k_copy(0, 0, True)
                q_copy(0, 0)
                body(0, new=True)
                with act.Fori(1, HEADS // 4 - 1) as i:
                    body(i)
                body(HEADS // 4 - 1, last=True)
                for u in range(NU):
                    probs_T(HEADS // 4, -1, u, False)

            load(cs[:, 0, :], cT, "c")
            load(kc[:], consts, "const")
            load(xs[:], x.rearrange("(t p) d -> p t d", p=P), "x")
            load(brow0, bias_rows[0:1, 0:5 * D].to_broadcast([P, 5 * D]).rearrange("p (r n) -> p r n", r=5), "bias0")
            load(rows[:, F_GATE0, :], bias_rows[0:1, 5 * D:6 * D].to_broadcast([P, D]), "biasg")
            load(gain0, gains[0:1, 0:2 * D].to_broadcast([P, 2 * D]).rearrange("p (r n) -> p r n", r=2), "gain0")
            load(convs[:], conv, "conv")
            load(keyT, keys[0], "keys0")
            load(fb[:], f_bias, "fb")
            act.wait_ge(ld["c"], 16)
            act.activation(cs[:, 1, :], cs[:, 0, :], ACT.Exp, scale=-1.0).then_inc(silu_e, 1)
            ada_first()
            ada0(C_ADA0, N_SQ, GATE)
            ada0(C_ADA0 + N_SQ, 2 * N_SQ, F_SHIFT)
            norm("mix0", hT, ld["x"], 16)
            in_proj()
            norm("ffn0", hT, x_mix[0], 4 * N_SQ, [0])
            first_scores(0)
            copies("ffn0", hT, [1, 2, 3])
            plain = [(1, STEPS // 2 - 2, None, 0)]
            soft(0)
            gelus(0, rest_scores(0), lambda: soft(1))
            act.wait_ge(x_ffn[0], 1)
            gelus(1, [(1, 14, lambda k: ada_pair(1, C_ADA1, SHIFT, k), 0)], lambda: soft(2))
            gelus(2, [(1, 2, lambda k: ada_pair(1, C_ADA1 + 28, F_GATE1, k), 0), (1, 12, None, 0)], lambda: soft(3))
            act.wait_ge(r_ok, NT)
            load(brow1, bias_rows[0:1, 6 * D:14 * D].to_broadcast([P, 8 * D]).rearrange("p (r n) -> p r n", r=8), "bias1")
            act.wait_ge(x_ffn[0], NT - 1)
            load(gain1, gains[0:1, 2 * D:5 * D].to_broadcast([P, 3 * D]).rearrange("p (r n) -> p r n", r=3), "gain1")
            gelus(3, early_work())
            act.wait_ge(x_ffn[0], NT)
            load(fw, f_w, "fw")
            late_work()
            load(keyT, keys[1], "keys1")
            attention()
            copies("att", hT)
            norm("ffn1", hT, x_mix[1], 4 * N_SQ, [0])
            first_scores(1)
            copies("ffn1", hT, [1, 2, 3])
            soft(4)
            gelus(4, rest_scores(1), lambda: soft(5))
            act.wait_ge(x_ffn[1], 1)
            load(rows[:, SHIFT, :], gains[0:1, 5 * D:6 * D].to_broadcast([P, D]), "gainf")
            gelus(5, plain, lambda: soft(6))
            gelus(6, plain, lambda: soft(7))
            act.wait_ge(x_ffn[1], FEW)
            gelus(7, one_by_one((lambda: squares("fin", range(FEW)), 1, 0), (None, 1, 0),
                                (lambda: roots("fin", slice(0, FEW), 1), 1, 0), (None, 11, 0)))
            act.wait_ge(x_ffn[1], NT)
            squares("fin", [FEW])
            roots("fin", slice(FEW, NT), 2)

        @block.vector
        def _(dve):
            me = Ticks(dve, dv)

            def silu():
                dve.wait_ge(silu_e, 1)
                me(dve.tensor_scalar(cs[:, 2, :], cs[:, 1, :], 1.0, None, ALU.add))
                me.sync()
                me(dve.reciprocal(cs[:, 1, :], cs[:, 2, :]))
                me.sync()
                me(dve.tensor_tensor(cs[:, 2, :], cs[:, 0, :], cs[:, 1, :], ALU.mult))
                me.sync()
                dve.tensor_copy(sB[:], cs[:, 2, :].unsqueeze(2).to_broadcast([P, KB, P])).then_inc(silu_b, 1)

            def finish_rows(plan, brow, gain):
                for row, b, const, _ in plan:
                    me(dve.scalar_tensor_tensor(rows[:, row, :], rows[:, row, :], const, brow[:, b, :], ALU.add, ALU.add))
                me.sync()
                for row, _, _, g in plan:
                    if g is not None:
                        me(dve.tensor_tensor(rows[:, row, :], rows[:, row, :], gain[:, g, :], ALU.mult))
                me.sync()

            def norm(name, a_row, b_row):
                dve.wait_ge(n_sq[name], NT)
                dve.tensor_scalar(stat[:, 0, :], stat[:, 0, :], 1.0 / D, EPS, ALU.mult, ALU.add).then_inc(n_ms[name], 1)
                dve.wait_ge(n_rt[name], 1)
                me(dve.reciprocal(stat[:, 0, :], stat[:, 1, :]))
                me.sync()
                for t in range(NT):
                    me(dve.scalar_tensor_tensor(hs[:, t, :], xs[:, t, :], stat[:, 0, t:t + 1], rows[:, a_row, :],
                                                ALU.mult, ALU.mult))
                    if t:
                        me.sync(1)
                        dve.tensor_tensor(hs[:, t - 1, :], hs[:, t - 1, :], rows[:, b_row, :], ALU.add).then_inc(n_h[name], 1)
                me.sync()
                dve.tensor_tensor(hs[:, NT - 1, :], hs[:, NT - 1, :], rows[:, b_row, :], ALU.add).then_inc(n_h[name], 1)

            def mean_squares(name, tiles, count):
                dve.wait_ge(n_sq[name], count)
                dve.tensor_scalar(stat[:, 0, tiles], stat[:, 0, tiles], 1.0 / D, EPS, ALU.mult, ALU.add).then_inc(n_ms[name], 1)

            def output(tiles, count):
                dve.wait_ge(n_rt["fin"], count)
                me(dve.reciprocal(stat[:, 0, tiles], stat[:, 1, tiles]))
                me.sync()
                dve.wait_ge(ld["gainf"], 16)
                for t in range(tiles.start, tiles.stop):
                    dve.scalar_tensor_tensor(xs[:, t, :], xs[:, t, :], stat[:, 0, t:t + 1], rows[:, SHIFT, :],
                                             ALU.mult, ALU.mult).then_inc(y_ok, 1)

            def mix_input(name, tiles, at=None):
                a_row, b_row = {"kv": (KV_SCALE, KV_SHIFT), "mix1": (SCALE, SHIFT)}[name]
                for t in tiles:
                    dst = hs[:, t if at is None else at, :]
                    me(dve.scalar_tensor_tensor(dst, xs[:, t, :], stat[:, 0, t:t + 1], rows[:, a_row, :],
                                                ALU.mult, ALU.mult))
                me.sync()
                for t in tiles:
                    dst = hs[:, t if at is None else at, :]
                    dve.tensor_tensor(dst, dst, rows[:, b_row, :], ALU.add).then_inc(n_h[name], 1)

            def early_work():
                def bias(plan, first=False):
                    if first:
                        dve.wait_ge(ld["bias1"], 16)
                        dve.wait_ge(ada_out[1], N_ADA[1])
                    for row, b, const in plan:
                        me(dve.scalar_tensor_tensor(rows[:, row, :], rows[:, row, :], const, brow1[:, b, :],
                                                    ALU.add, ALU.add))
                    me.sync()

                def bias_2():
                    bias([(GATE, 2, 1.0), (F_SHIFT, 5, 0.0), (F_SCALE, 6, 1.0), (F_GATE1, 7, 1.0)])
                    mean_squares("kv", slice(0, FEW), FEW)

                def gain_rows():
                    dve.wait_ge(ld["gain1"], 16)
                    for row, g in ((SCALE, 1), (KV_SCALE, 0), (F_SCALE, 2)):
                        me(dve.tensor_tensor(rows[:, row, :], rows[:, row, :], gain1[:, g, :], ALU.mult))
                    me.sync()

                def kv_01():
                    dve.wait_ge(n_rt["kv"], 1)
                    me(dve.reciprocal(stat[:, 0, 0:FEW], stat[:, 1, 0:FEW]))
                    me.sync()
                    mix_input("kv", [0, 1])

                def mix(tiles):
                    dve.wait_ge(n_tr["kv"], 2 * tiles[-1] + 2)
                    mix_input("mix1", tiles)
                return one_by_one(
                    (lambda: bias([(SHIFT, 0, 0.0), (SCALE, 1, 1.0), (KV_SHIFT, 3, 0.0), (KV_SCALE, 4, 1.0)], True), 1, 4),
                    (bias_2, 1, 4), (gain_rows, 1, 3), (kv_01, 1, 3), (lambda: mix_input("kv", [2]), 1, 1),
                    (None, 1, 0), (lambda: mix([0, 1]), 1, 2), (lambda: mix([2]), 1, 1), (None, 6, 0))

            def late_work():
                mean_squares("kv", slice(FEW, NT), NT)
                dve.wait_ge(n_rt["kv"], 2)
                me(dve.reciprocal(stat[:, 0, FEW:NT], stat[:, 1, FEW:NT]))
                me.sync()
                mix_input("kv", [FEW])
                dve.wait_ge(n_tr["mix1"], 2 * FEW)
                mix_input("mix1", [FEW], 0)

            def in_proj():
                me(dve.memset(cu[:, :, 0:2], 0.0))
                me.sync()

                def body(i, first):
                    for jp in range(2):
                        J = 4 * i + 2 * jp
                        n = C_IN + 3 * jp
                        me(dve.tensor_copy(taps[:], convs[:, bass.ds(J, 2), :]))
                        w_done(dve, n + 1, 3 * i)
                        for jj in range(2):
                            dve.wait_ge(c_out, J + jj + 1)
                            dve.tensor_tensor(cu[:, jj, 2:2 + S], ps[2 + jj], c_s[:, jj, :], ALU.mult).then_inc(cu_ok, 1)
                        dve.wait_ge(cu_ok, J + 2)
                        me.sync()
                        for jj in range(2):
                            me(dve.tensor_scalar(z_s[:, jj, :], cu[:, jj, 0:S], taps[:, jj, 0:1], None, ALU.mult))
                        for w in (1, 2):
                            for jj in range(2):
                                me.sync(1)
                                me(dve.scalar_tensor_tensor(z_s[:, jj, :], cu[:, jj, w:w + S], taps[:, jj, w:w + 1],
                                                            z_s[:, jj, :], ALU.mult, ALU.add))
                        w_done(dve, n + 2, 3 * i)
                        me.sync()
                        for jj in range(2):
                            dve.tensor_tensor(gT[:, bass.ds(J + jj, 1), :].squeeze(1), ps[4 + jj], z_s[:, jj, :],
                                              ALU.mult).then_inc(g_ok, 1)
                body(0, True)
                body(1, False)

            def add_projection(L, c0, gate_row):
                def body(i, first):
                    for s in range(2):
                        w_done(dve, c0 + s, i)
                        cols = bass.ds((2 * i + s) * CW, CW)
                        done = 2 * NT * i + NT * s
                        if not first:
                            dve.wait_ge(x_mix[L], done - NT)
                        for t in range(NT):
                            dve.tensor_tensor(y_s[:, s, t, :], ps[4 * s + t][:, 0:CW], rows[:, gate_row, cols],
                                              ALU.mult).then_inc(y_in[L], 1)
                        for t in range(NT):
                            dve.wait_ge(y_in[L], done + t + 1)
                            dve.tensor_tensor(xs[:, t, cols], xs[:, t, cols], y_s[:, s, t, :], ALU.add).then_inc(x_mix[L], 1)
                peeled(dve, N_SQ // 2, body)

            def list_steps(g):
                return 5 * g + 3

            def head_steps(g):
                return 5 * g + 11

            def route_lists(T, i, g):
                r = scratch_for(T)
                stage, tv, tif, tv4, ti4 = r.stage[:, 0:g, :], r.tv, r.tif, r.tv4[:, 0:g, :], r.ti4[:, 0:g, :]
                if T % NT < 2:
                    dve.wait_ge(s_out[T // NT], g * i + (g + LISTS * (T % NT)))
                me(dve.tensor_copy(stage, sc[:, T % NT, bass.ds(g * i, g), :]))
                top16([stage[:, l, :] for l in range(g)], tv4, ti4)
                me(dve.tensor_copy(tv[:, bass.ds(g * i, g), :], tv4))
                me(dve.tensor_copy(tif[:, bass.ds(g * i, g), :], ti4))
                me.sync()

            def route_heads(T, i, g):
                r, n = scratch_for(T), g * TOPK
                full = [P, g, TOPK, TOPK]
                cand, pick1, pick2, bv4 = r.cand[:, 0:g], r.pick1[:, 0:n, :], r.pick2[:, 0:n, :], r.bv4[:, 0:g, :]
                bp4, ra4, rb4, e1, e2 = (m[:, 0:n] for m in (r.bp4, r.ra4, r.rb4, r.e1, r.e2))
                by_head = r.tv.rearrange("p (h c) k -> p h c k", c=2)
                idx_by_head = r.tif.rearrange("p (h c) k -> p h c k", c=2)
                hh = bass.ds(g * i, g)
                me(dve.tensor_tensor(cand, by_head[:, hh, 0, :].unsqueeze(3).to_broadcast(full),
                                     by_head[:, hh, 1, :].unsqueeze(2).to_broadcast(full), ALU.add))
                top16([r.candf[:, l, :] for l in range(g)], bv4, bp4.rearrange("p (l k) -> p l k", l=g))
                me(dve.tensor_copy(bs[:, hh, :], bv4))
                me(dve.tensor_scalar(ra4, bp4, 4, None, ALU.logical_shift_right))
                me(dve.tensor_scalar(rb4, bp4, TOPK - 1, None, ALU.bitwise_and))
                for pick, rank in ((pick1, ra4), (pick2, rb4)):
                    me.sync(0 if pick is pick1 else 1)
                    me(dve.tensor_tensor(pick, iota.unsqueeze(1).to_broadcast([P, n, TOPK]),
                                         rank.unsqueeze(2).to_broadcast([P, n, TOPK]), ALU.is_equal))
                for c, pick in enumerate((pick1, pick2)):
                    me.sync(1)
                    p4 = pick.rearrange("p (h k) a -> p h k a", h=g)
                    me(dve.tensor_tensor(p4, p4, idx_by_head[:, hh, c, :].unsqueeze(2).to_broadcast(full), ALU.mult))
                for pick, e in ((pick1, e1), (pick2, e2)):
                    me.sync(1)
                    me(dve.tensor_reduce(e, pick, AX_X, ALU.add))
                me.sync()
                me(dve.scalar_tensor_tensor(idx[:, T % 2, bass.ds(n * i, n)], e1, float(NK), e2, ALU.mult, ALU.add))
                me.sync()

            def route_gates(T):
                dve.tensor_tensor(bd, bs, bs[:, :, 0:1].to_broadcast([P, PH, TOPK]), ALU.subtract).then_inc(r_d, 1)
                dve.wait_ge(r_e, T + 1)
                me(dve.tensor_reduce(gsum[:, 0, :], bd, AX_X, ALU.add))
                me.sync()
                me(dve.reciprocal(gsum[:, 1, :], gsum[:, 0, :]))
                me.sync()
                dve.tensor_tensor(gates[:, T % 2, :].rearrange("p (h k) -> p h k", h=PH), bd,
                                  gsum[:, 1, :].unsqueeze(2).to_broadcast([P, PH, TOPK]), ALU.mult).then_inc(r_ok, 1)
                dve.wait_ge(r_ok, T + 1)

            def finish_gate():
                dve.wait_ge(ld["biasg"], 16)
                for n in range(N_GATE):
                    w_done(dve, C_GATE0 + n)
                    cols = rows[:, F_GATE0, n * CW:(n + 1) * CW]
                    dve.scalar_tensor_tensor(cols, ps[n][:, 0:CW], 1.0, cols, ALU.add, ALU.add).then_inc(gate_out, 1)

            def route(T):
                with dve.Fori(0, 2) as i:
                    me.enter(i, 2 * list_steps(4) + head_steps(4))
                    route_lists(T, 2 * i, 4)
                    route_lists(T, 2 * i + 1, 4)
                    route_heads(T, i, 4)
                me.leave(2)
                route_gates(T)

            def routing_of(T):
                late = T % NT == 1
                return ([(1, 2, None, 0)] * late +
                        [(1, LISTS // 2, lambda k: route_lists(T, k, 2), list_steps(2)),
                         (1, PH // 2, lambda k: route_heads(T, k, 2), head_steps(2))] +
                        [(1, 2, None, 0)] * (not late))

            def top16(lists, best, where):
                def settle():
                    me.sync()
                    dve.nop(nofuse=True)
                for r in range(2):
                    w = slice(8 * r, 8 * r + 8)
                    settle()
                    for l, values in enumerate(lists):
                        me(dve.max(best[:, l, w], values))
                    settle()
                    for l, values in enumerate(lists):
                        me(dve.max_index(where[:, l, w], best[:, l, w], values))
                    if r == 0:
                        settle()
                        for l, values in enumerate(lists):
                            me(dve.match_replace(values, best[:, l, w], values, LOWEST))
                me.sync()

            def dot(T, n, r):
                buf = ring[:, HALF * n + r, :]
                dve.tensor_tensor_reduce(buf, buf, hs[:, T % NT, :], 1.0, 0.0, ALU.mult, ALU.add,
                                         dots[:, n, r:r + 1]).then_inc(u_used[n], 1)

            def first_dots(T):
                dve.wait_ge(r_ok, T + 1)
                dve.wait_ge(u_got[0], 16 * HALF * (T * (STEPS // 2) + 1))
                for r in range(HALF):
                    dot(T, 0, r)

            def experts(T, segments, last=None):
                t, base = T % NT, T * (STEPS // 2)
                g = gates[:, T % 2, :]
                eq = (in_rows.eq, in_hT.eq, in_hT.eq, scf[:, 0:D])[t] if T < NT else (in_rows if t == 0 else in_hT).eq
                dve.wait_ge(n_hT[f"ffn{T // NT}"], 2 * NT)
                for b in (6, 7):
                    me(dve.memset(ps[b], 0.0))
                if t == 0:
                    first_dots(T)
                me.sync()

                def weigh(n, f, slot):
                    dve.wait_ge(act_ok[n], f + 1)
                    dve.tensor_tensor(coef[:, n, :], acts[:, n, :], g[:, bass.ds(slot, HALF)],
                                      ALU.mult).then_inc(coef_ok[n], 1)

                def add(n, f, r, first):
                    if r:
                        dve.wait_ge(v_used[n], BY_DVE * f + r)
                    elif not first:
                        dve.wait_ge(v_used[1 - n], BY_DVE * (f + n))
                    dve.scalar_tensor_tensor(acc, ring[:, 8 + HALF * n + r, :], coef[:, n, r:r + 1], acc,
                                             ALU.mult, ALU.add).then_inc(v_used[n], 1)

                def step(nu, fu, nv, fv, slot, first=False):
                    dve.wait_ge(u_got[nu], 16 * HALF * (fu + 1))
                    dot(T, nu, 0)
                    weigh(nv, fv, slot)
                    dot(T, nu, 1)
                    dve.wait_ge(v_got[nv], 16 * HALF * (fv + 1))
                    dve.wait_ge(coef_ok[nv], fv + 1)
                    add(nv, fv, 0, first)
                    dot(T, nu, 2)
                    add(nv, fv, 1, first)
                    dot(T, nu, 3)

                step(1, base, 0, base, 0, first=True)
                step(0, base + 1, 1, base, HALF)
                def turn(i, _):
                    step(1, i + base, 0, i + base, 2 * HALF * i)
                    step(0, i + (base + 1), 1, i + base, 2 * HALF * i + HALF)
                window(dve, turn, segments, me)
                if last:
                    last()
                end = base + STEPS // 2 - 1
                step(1, end, 0, end, SLOTS - 2 * HALF)
                weigh(1, end, SLOTS - HALF)
                dve.wait_ge(v_got[1], 16 * HALF * (end + 1))
                dve.wait_ge(coef_ok[1], end + 1)
                for r in range(BY_DVE):
                    add(1, end, r, False)
                if t < NT - 1:
                    first_dots(T + 1)
                dve.wait_ge(v_used[1], BY_DVE * (end + 1))
                me(dve.tensor_tensor(eq, acc, rows[:, F_GATE[T // NT], :], ALU.mult))
                me.sync()
                me(dve.tensor_tensor(xs[:, t, :], xs[:, t, :], eq, ALU.add))
                me.sync()
                dve.wait_ge(v_used_pe[1], end + 1)
                me(dve.tensor_tensor(eq, acc_pe, rows[:, F_GATE[T // NT], :], ALU.mult))
                me.sync()
                dve.tensor_tensor(xs[:, t, :], xs[:, t, :], eq, ALU.add).then_inc(x_ffn[T // NT], 1)
                dve.wait_ge(x_ffn[T // NT], t + 1)

            def forget():
                me(dve.memset(aux_l, 1.0))
                me(dve.memset(kq_head[1][32:64], 0.0))
                dve.wait_ge(f_done, 1)
                dve.wait_ge(ld["fb"], 16)
                dve.tensor_scalar(cum, ps[0][0:FR, :], fb[:], None, ALU.add).then_inc(f_z, 1)
                dve.wait_ge(f_l, 1)
                dve.wait_ge(f_z, 1)
                me(dve.scalar_tensor_tensor(aux_b, cum, 0.0, aux_r, ALU.min, ALU.subtract))
                me.sync()
                me(dve.tensor_tensor_scan(cum, aux_l, aux_b, 0.0, ALU.mult, ALU.add))
                me.sync()
                me(dve.tensor_copy(aux_r, cum))
                me(dve.tensor_copy(aux_b, cum))
                me.sync()
                for n in (0, 64):
                    me(dve.memset(aux_b[n:n + 32, :], -1.0))
                    me(dve.memset(aux_r[n + 32:n + 48, :], 1.0))
                me.sync()
                for kq, terms in zip(kq_head, TERMS):
                    for s in range(2):
                        me(dve.tensor_copy(kq[terms, s, 0, :], aux_r[terms, :]))
                me.sync()

            def attention():
                def scores(i, c, u):
                    n = 4 * i + c
                    dve.wait_ge(a_s, NU * n + u + 1)
                    for t in UNITS[u]:
                        diagonal = ps[2 + u][:, U_COL[t] + t * P:U_COL[t] + (t + 1) * P]
                        me(dve.tensor_tensor(diagonal, diagonal, mask, ALU.add))
                    me.sync()
                    for t in UNITS[u]:
                        dve.reduce_max(amax[:, c % 2, t:t + 1], ps[2 + u][:, U_COL[t]:U_COL[t] + (t + 1) * P], AX_X,
                                       negate=True).then_inc(a_max, 1)

                def aux(i, c, new=False):
                    n = 4 * i + c
                    rows48 = TERMS[c % 2]
                    if not (new and c < 4):
                        dve.wait_ge(a_s, NU * n - 3 * NU)
                    dve.tensor_tensor(kq_head[c % 2][rows48, c // 2 % 2, 1, :], aux_b[rows48, :],
                                      kc[rows48, bass.ds(K_SEL + n, 1)].to_broadcast([48, S]), ALU.mult).then_inc(aux_ok, 1)

                def inverse(i, c):
                    dve.wait_ge(a_exp, 4 * (4 * i + c) + 4)
                    me(dve.reciprocal(ainv[:, c % 2, :], asum[:, c % 2, :]))

                def finish(i, c):
                    n = 4 * i + c
                    dve.wait_ge(a_pv, NU * n + NU)
                    dve.tensor_tensor(hs[:, :, bass.ds(n * HD, HD)],
                                      ps[(1, 5)[c % 2]][:, 0:NT * HD].rearrange("p (t d) -> p t d", t=NT),
                                      ainv[:, c % 2, :].unsqueeze(2).to_broadcast([P, NT, HD]), ALU.mult).then_inc(a_o, 1)

                def body(i, new=False, last=False):
                    for c in range(4):
                        scores(i, c, 0)
                        if not (new and c == 0):
                            inverse(i, c - 1)
                        scores(i, c, 1)
                        if not (new and c < 2):
                            finish(i, c - 2)
                        if not (last and c == 3):
                            aux(i, c + 1, new)
                        scores(i, c, 2)
                aux(0, 0, True)
                body(0, new=True)
                with dve.Fori(1, HEADS // 4 - 1) as i:
                    me.enter(i - 1, 20)
                    body(i)
                me.leave(HEADS // 4 - 2)
                body(HEADS // 4 - 1, last=True)
                inverse(HEADS // 4, -1)
                finish(HEADS // 4, -2)
                me.sync()
                finish(HEADS // 4, -1)

            dve.wait_ge(ld["c"], 16)
            silu()
            dve.wait_ge(ld["bias0"], 16)
            dve.wait_ge(ld["gain0"], 16)
            dve.wait_ge(ada_out[0], 12)
            finish_rows([(SHIFT, 0, 0.0, None), (SCALE, 1, 1.0, 0), (GATE, 2, 1.0, None)], brow0, gain0)
            dve.wait_ge(ld["x"], 16)
            norm("mix0", SCALE, SHIFT)
            dve.wait_ge(ada_out[0], N_ADA[0])
            finish_rows([(F_SHIFT, 3, 0.0, None), (F_SCALE, 4, 1.0, 1)], brow0, gain0)
            dve.wait_ge(ld["conv"], 16)
            in_proj()
            add_projection(0, C_OUT, GATE)
            norm("ffn0", F_SCALE, F_SHIFT)
            dve.wait_ge(ld["const"], 16)
            route(0)
            def last_work():
                finish_gate()
                route_gates(1)
            experts(0, routing_of(1), last_work)
            for T in range(1, NT - 1):
                experts(T, routing_of(T + 1), lambda: route_gates(T + 1))
            experts(NT - 1, early_work())
            late_work()
            forget()
            attention()
            add_projection(1, C_WO, GATE)
            norm("ffn1", F_SCALE, F_SHIFT)
            route(NT)
            for T in range(NT, 2 * NT - 1):
                experts(T, routing_of(T + 1), lambda: route_gates(T + 1))
            experts(2 * NT - 1, one_by_one((None, 1, 0), (lambda: mean_squares("fin", slice(0, FEW), FEW), 1, 0),
                                           (None, 1, 0), (lambda: output(slice(0, FEW), 1), 1, 1), (None, 10, 0)))
            mean_squares("fin", slice(FEW, NT), NT)
            output(slice(FEW, NT), 2)

        @block.gpsimd
        def _(pool):
            def gather(kind, T, n, f, slot, first=False):
                table, at, ids, got, copied = (
                    (tables[2 * (T // NT)], 0, idx_u, u_got, ix_u) if kind == "u" else
                    (tables[2 * (T // NT) + 1], 8, idx_v, v_got, ix_v))
                if not first:
                    if kind == "u":
                        pool.wait_ge(u_used[n], HALF * f)
                    else:
                        pool.wait_ge(v_used[n], BY_DVE * f)
                        pool.nop(nofuse=True)
                        pool.wait_ge(v_used_pe[n], f)
                    pool.nop(nofuse=True)
                pool.tensor_copy(ids[:, n, :], idx[:, T % 2, bass.ds(slot, HALF)]).then_inc(copied, 1)
                pool.wait_ge(copied, 2 * f + (n + 1))
                pool.nop(nofuse=True)
                for r in range(HALF):
                    pool.indirect_dma_start(ring[:, at + HALF * n + r, :], None, table,
                                            bass.IndirectOffsetOnAxis(ap=ids[:, n, r:r + 1], axis=0)).then_inc(got[n], 16)

            def tile(T):
                base = T * (STEPS // 2)
                new = T == 0
                pool.wait_ge(r_ok, T + 1)
                gather("u", T, 0, base, 0, new)
                gather("u", T, 1, base, HALF, new)
                gather("v", T, 0, base, 0, new)
                gather("u", T, 0, base + 1, 2 * HALF)
                gather("v", T, 1, base, HALF, new)
                with pool.Fori(1, STEPS // 2 - 1) as i:
                    gather("u", T, 1, i + base, 2 * HALF * i + HALF)
                    gather("v", T, 0, i + base, 2 * HALF * i)
                    gather("u", T, 0, i + (base + 1), 2 * HALF * i + 2 * HALF)
                    gather("v", T, 1, i + base, 2 * HALF * i + HALF)
                last = base + STEPS // 2 - 1
                gather("u", T, 1, last, SLOTS - HALF)
                gather("v", T, 0, last, SLOTS - 2 * HALF)
                gather("v", T, 1, last, SLOTS - HALF)

            for T in range(NT):
                tile(T)
            pool.wait_ge(x_ffn[0], NT)
            pool.wait_ge(n_hT["mix1"], 2 * FEW)
            pool.tensor_copy(hqT[:, :, 0:FEW * P], hq_early).then_inc(hq_ok, 1)
            for T in range(NT, 2 * NT):
                tile(T)


INPUTS = ["x", "cT", "consts", "conv", "f_w", "f_bias", "bias_rows", "gains", "keys", "wfirst", "wstream",
          "u0", "v0", "u1", "v1"]


def kernel(**inputs):
    import numpy as np
    import concourse.bacc as bacc
    from concourse.bass_utils import run_bass_kernel_spmd as run

    a = {k: np.asarray(v) for k, v in inputs.items()}

    def chunks(w):
        return w.reshape(KB, P, -1, CW).transpose(2, 1, 0, 3).reshape(-1, P, KB * CW)

    w_in = a["a_w_in"][0].reshape(D, 3, N_SQ, CW)[:, [1, 2, 0]].transpose(0, 2, 1, 3).reshape(D, 3 * D)
    w_k, w_v, w_f = a["kv_w"][:, 0:D], a["kv_w"][:, D:2 * D], a["kv_w"][:, 2 * D:]
    w_kq = np.stack([w_k.reshape(D, KB, P), a["b_w_q"][0].reshape(D, KB, P)], axis=2).reshape(D, 2 * D)
    mix_ada, ffn_ada = a["mix_ada_w"][0], a["ffn_ada_w"][0]
    stream = [mix_ada[:, 2 * D:], ffn_ada[:, 0:2 * D], w_in, a["a_w_out"][0], a["peer_w_q"][0], a["peer_w_q"][0],
              ffn_ada[:, 2 * D:],
              a["mix_ada_w"][1], a["kv_ada_w"], a["ffn_ada_w"][1], w_v, w_v, w_kq, a["b_w_o"][0],
              a["peer_w_q"][1], a["peer_w_q"][1]]
    consts = np.zeros((P, K_COLS), np.float32)
    consts[:, K_ID:K_ID + P] = np.eye(P)
    consts[:, K_MASK:K_MASK + P] = np.where(np.arange(P)[None, :] <= np.arange(P)[:, None], 0.0, -1.0e30)
    consts[:, K_IOTA:K_IOTA + TOPK] = np.arange(TOPK)
    for n in (0, 32, 64, 96):
        consts[n:n + HEADS, K_SEL:K_SEL + HEADS] = np.eye(HEADS)
    consts[:, K_ONE] = 1.0
    arrays = {
        "x": a["x"][0],
        "cT": a["c"].reshape(KB, P).T,
        "consts": consts,
        "conv": a["a_conv"][0].reshape(3, KB, P).transpose(2, 1, 0),
        "f_w": np.tile(w_f.reshape(KB, P, HEADS).transpose(1, 0, 2), (1, 1, FR // HEADS)),
        "f_bias": np.tile(a["f_bias"].reshape(HEADS, 1), (FR // HEADS, 1)),
        "bias_rows": np.concatenate([a["mix_ada_b"][0], a["ffn_ada_b"][0], a["mix_ada_b"][1], a["kv_ada_b"],
                                     a["ffn_ada_b"][1]]).reshape(1, -1),
        "gains": np.concatenate([a["mix_norm"][0], a["ffn_norm"][0], a["kv_norm"], a["mix_norm"][1],
                                 a["ffn_norm"][1], a["final_norm"]]).reshape(1, -1),
        "keys": a["peer_sub_keys"].reshape(2, LISTS * NK, DK).transpose(0, 2, 1),
        "wfirst": chunks(mix_ada[:, 0:2 * D]),
        "wstream": np.concatenate([chunks(w) for w in stream]),
        "u0": a["peer_u"][0], "v0": a["peer_v"][0], "u1": a["peer_u"][1], "v1": a["peer_v"][1],
    }
    nc = bacc.Bacc("TRN2", target_bir_lowering=False, num_devices=1)
    arrays = {f"in_{k}": np.ascontiguousarray(arrays[k]) for k in INPUTS}
    aps = [nc.dram_tensor(k, v.shape, mybir.dt.from_np(v.dtype), kind="ExternalInput").ap() for k, v in arrays.items()]
    out = nc.dram_tensor("out_y", (S, D), F32, kind="ExternalOutput").ap()
    bass_trunk(nc, *aps[:11], aps[11:], out)
    r = run(nc, [arrays], core_ids=[0])
    return r.results[0]["out_y"].reshape(1, S, D)
```
